# Optimizing a Trainium2 kernel written in Bass

```python
import jax, jax.numpy as jnp
from jax import lax
import numpy as np

D_MODEL = 2048
BATCH = 1
SEQ = 256
DEPTH = 1
DEC_BATCH = 8
DEC_SEQ = 1
PAST_LEN = 1024
PAGE_SIZE = 128

SB_HEADS = 8
SB_HEAD_DIM = 128
SB_WIDTH = SB_HEADS * SB_HEAD_DIM
SB_BIAS_INIT = -8.0
Q_BLOCK = 128
GLA_HEADS = 4
GLA_DK = 128
GLA_DV = 256
GLA_KW = GLA_HEADS * GLA_DK
GLA_VW = GLA_HEADS * GLA_DV
GLA_GATE_RANK = 16
GLA_GATE_NORM = 16.0
GLA_CHUNK = 64
MIX_WIDTH = SB_WIDTH + GLA_VW
IN_SPLIT_POINTS = (SB_WIDTH, 2 * SB_WIDTH, 3 * SB_WIDTH,
                   3 * SB_WIDTH + GLA_KW, 3 * SB_WIDTH + 2 * GLA_KW,
                   3 * SB_WIDTH + 2 * GLA_KW + GLA_VW,
                   3 * SB_WIDTH + 2 * GLA_KW + 2 * GLA_VW)
IN_WIDTH = 3 * SB_WIDTH + 2 * GLA_KW + 2 * GLA_VW + GLA_GATE_RANK
D_FF = -(-(8 * D_MODEL) // (3 * 256)) * 256
N_MOD = 6
EPS = 1e-6

kernel_name = "stickbreak_gla_hymba_step"

def rmsnorm(x, g):
    xf = x.astype(jnp.float32)
    y = xf * lax.rsqrt(jnp.mean(xf * xf, axis=-1, keepdims=True) + EPS)
    return (y * g.astype(jnp.float32)).astype(x.dtype)

def sb_block(q, k, v, bias, q_pos, k_pos):
    z = jnp.einsum('bhqd,bhkd->bhqk', q.astype(jnp.float32), k.astype(jnp.float32)) * (SB_HEAD_DIM ** -0.5)
    z = z + bias.astype(jnp.float32)[None, :, None, None]
    mask = k_pos[None, :] < q_pos[:, None]
    log_beta = jax.nn.log_sigmoid(z)
    log_keep = jnp.where(mask, jax.nn.log_sigmoid(-z), 0.0)
    tail = lax.cumsum(log_keep, axis=3, reverse=True) - log_keep
    a = jnp.where(mask, jnp.exp(log_beta + tail), 0.0)
    return jnp.einsum('bhqk,bhkd->bhqd', a, v.astype(jnp.float32))

def sb_prompt(q, k, v, bias):
    B, H, S, dh = q.shape
    nb = S // Q_BLOCK
    qb = q.reshape(B, H, nb, Q_BLOCK, dh).transpose(2, 0, 1, 3, 4)
    pos = jnp.arange(S)
    qpos = pos.reshape(nb, Q_BLOCK)
    out = lax.map(lambda a: sb_block(a[0], k, v, bias, a[1], pos), (qb, qpos))
    return out.transpose(1, 2, 0, 3, 4).reshape(B, H, S, dh)

def gla_chunked(q, k, v, g, s0, chunk):
    B, H, T, dk = q.shape
    dv = v.shape[-1]
    n = T // chunk

    def to_chunks(a):
        return a.astype(jnp.float32).reshape(B, H, n, chunk, a.shape[-1]).transpose(2, 0, 1, 3, 4)

    qc, kc, vc, gc = to_chunks(q), to_chunks(k), to_chunks(v), to_chunks(g)
    causal = jnp.tril(jnp.ones((chunk, chunk), bool))[:, :, None]

    def step(S, inp):
        qi, ki, vi, gi = inp
        b = jnp.cumsum(gi, axis=2)
        o_inter = jnp.einsum('bhtd,bhdv->bhtv', qi * jnp.exp(b), S)
        diff = b[:, :, :, None, :] - b[:, :, None, :, :]
        decay = jnp.exp(jnp.where(causal, diff, -jnp.inf))
        att = jnp.einsum('bhtd,bhsd,bhtsd->bhts', qi, ki, decay)
        o = o_inter + jnp.einsum('bhts,bhsv->bhtv', att, vi)
        b_last = b[:, :, -1:, :]
        S_new = jnp.exp(b_last[:, :, 0, :])[..., None] * S + \
            jnp.einsum('bhsd,bhsv->bhdv', ki * jnp.exp(b_last - b), vi)
        return S_new, o

    S_fin, o = lax.scan(step, s0.astype(jnp.float32), (qc, kc, vc, gc))
    o = o.transpose(1, 2, 0, 3, 4).reshape(B, H, T, dv)
    return o, S_fin

def token_mixer(h, w_in, b_sb, w_gate_up, b_gate, g_sb_out, g_gla_out, w_out, k_past, v_past, s0):
    B, T, _ = h.shape
    proj = h @ w_in
    q_sb, k_sb, v_sb, q_g, k_g, v_g, r_g, g_low = jnp.split(proj, IN_SPLIT_POINTS, axis=-1)

    def to_heads(a, nh):
        return a.reshape(B, T, nh, -1).transpose(0, 2, 1, 3)

    k_rows = k_sb.reshape(B, T, SB_HEADS, SB_HEAD_DIM)
    v_rows = v_sb.reshape(B, T, SB_HEADS, SB_HEAD_DIM)
    q_h = to_heads(q_sb, SB_HEADS)
    if k_past is None:
        o_sb = sb_prompt(q_h, to_heads(k_sb, SB_HEADS), to_heads(v_sb, SB_HEADS), b_sb)
        s0 = jnp.zeros((B, GLA_HEADS, GLA_DK, GLA_DV), jnp.float32)
        gla_chunk = min(GLA_CHUNK, T)
    else:
        past_len = k_past.shape[1]
        k_all = jnp.concatenate([k_past.astype(h.dtype), k_rows], axis=1).transpose(0, 2, 1, 3)
        v_all = jnp.concatenate([v_past.astype(h.dtype), v_rows], axis=1).transpose(0, 2, 1, 3)
        o_sb = sb_block(q_h, k_all, v_all, b_sb, past_len + jnp.arange(T), jnp.arange(past_len + T))
        gla_chunk = T
    o_sb = rmsnorm(o_sb.astype(h.dtype).transpose(0, 2, 1, 3), g_sb_out).reshape(B, T, SB_WIDTH)

    log_alpha = jax.nn.log_sigmoid((g_low @ w_gate_up + b_gate).astype(jnp.float32)) / GLA_GATE_NORM
    o_g, s_new = gla_chunked(to_heads(q_g, GLA_HEADS) * (GLA_DK ** -0.5), to_heads(k_g, GLA_HEADS),
                             to_heads(v_g, GLA_HEADS), to_heads(log_alpha, GLA_HEADS), s0, gla_chunk)
    o_g = rmsnorm(o_g.astype(h.dtype).transpose(0, 2, 1, 3), g_gla_out).reshape(B, T, GLA_VW)
    o_g = o_g * jax.nn.silu(r_g)

    out = jnp.concatenate([o_sb, o_g], axis=-1) @ w_out
    return out, k_rows, v_rows, s_new.astype(h.dtype)

def decoder_layer(x, c, w_ada, b_ada, g_pre_mix, w_in, b_sb, w_gate_up, b_gate, g_sb_out, g_gla_out,
                  w_out, g_post_mix, g_pre_ffn, w_ffn_gate, w_ffn_up, w_ffn_down, g_post_ffn,
                  k_past, v_past, s0):
    mod = (jax.nn.silu(c) @ w_ada + b_ada)[:, None, :]
    sh1, sc1, gt1, sh2, sc2, gt2 = jnp.split(mod, N_MOD, axis=-1)
    h = rmsnorm(x, g_pre_mix) * (1.0 + sc1) + sh1
    m, k_rows, v_rows, s_new = token_mixer(h, w_in, b_sb, w_gate_up, b_gate, g_sb_out, g_gla_out, w_out,
                                           k_past, v_past, s0)
    x = x + gt1 * rmsnorm(m, g_post_mix)
    h = rmsnorm(x, g_pre_ffn) * (1.0 + sc2) + sh2
    f = (jax.nn.silu(h @ w_ffn_gate) * (h @ w_ffn_up)) @ w_ffn_down
    x = x + gt2 * rmsnorm(f, g_post_ffn)
    return x, k_rows, v_rows, s_new

def setup_inputs(seed: int = 0) -> dict:
    key = jax.random.key(seed)
    ks = jax.random.split(key, 24)
    f32 = jnp.float32
    n_pages = PAST_LEN // PAGE_SIZE
    n_used = DEC_BATCH * n_pages
    n_pool = n_used + n_used // 4

    def nrm(k, shape, scale):
        return jax.random.normal(k, shape, f32) * scale

    def gain(k, n):
        return 1.0 + 0.05 * jax.random.normal(k, (DEPTH, n), f32)

    page_table = jax.random.permutation(ks[6], n_pool)[:n_used].reshape(DEC_BATCH, n_pages).astype(jnp.int32)
    return {
        "x_prompt": nrm(ks[0], (BATCH, SEQ, D_MODEL), 1.0),
        "x_sample": nrm(ks[1], (DEC_BATCH, DEC_SEQ, D_MODEL), 1.0),
        "c_prompt": nrm(ks[2], (BATCH, D_MODEL), 1.0),
        "c_sample": nrm(ks[3], (DEC_BATCH, D_MODEL), 1.0),
        "cache_k": nrm(ks[4], (DEPTH, n_pool, PAGE_SIZE, SB_HEADS, SB_HEAD_DIM), 1.0),
        "cache_v": nrm(ks[5], (DEPTH, n_pool, PAGE_SIZE, SB_HEADS, SB_HEAD_DIM), 1.0),
        "page_table": page_table,
        "state_gla": nrm(ks[7], (DEPTH, DEC_BATCH, GLA_HEADS, GLA_DK, GLA_DV), 0.1),
        "w_ada": nrm(ks[8], (DEPTH, D_MODEL, N_MOD * D_MODEL), 0.5 * D_MODEL ** -0.5),
        "b_ada": nrm(ks[9], (DEPTH, N_MOD * D_MODEL), 0.02),
        "g_pre_mix": gain(ks[10], D_MODEL),
        "w_in": nrm(ks[11], (DEPTH, D_MODEL, IN_WIDTH), D_MODEL ** -0.5),
        "b_sb": SB_BIAS_INIT + 0.1 * jax.random.normal(ks[23], (DEPTH, SB_HEADS), f32),
        "w_gate_up": nrm(ks[12], (DEPTH, GLA_GATE_RANK, GLA_KW), GLA_GATE_RANK ** -0.5),
        "b_gate": nrm(ks[13], (DEPTH, GLA_KW), 0.1),
        "g_sb_out": gain(ks[14], SB_HEAD_DIM),
        "g_gla_out": gain(ks[15], GLA_DV),
        "w_out": nrm(ks[16], (DEPTH, MIX_WIDTH, D_MODEL), MIX_WIDTH ** -0.5),
        "g_post_mix": gain(ks[17], D_MODEL),
        "g_pre_ffn": gain(ks[18], D_MODEL),
        "w_ffn_gate": nrm(ks[19], (DEPTH, D_MODEL, D_FF), D_MODEL ** -0.5),
        "w_ffn_up": nrm(ks[20], (DEPTH, D_MODEL, D_FF), D_MODEL ** -0.5),
        "w_ffn_down": nrm(ks[21], (DEPTH, D_FF, D_MODEL), D_FF ** -0.5),
        "g_post_ffn": gain(ks[22], D_MODEL),
    }

def reference(x_prompt, x_sample, c_prompt, c_sample, cache_k, cache_v, page_table, state_gla,
              w_ada, b_ada, g_pre_mix, w_in, b_sb, w_gate_up, b_gate, g_sb_out, g_gla_out, w_out,
              g_post_mix, g_pre_ffn, w_ffn_gate, w_ffn_up, w_ffn_down, g_post_ffn):
    yp, ys = x_prompt, x_sample
    dec_b = page_table.shape[0]
    kp_l, vp_l, sp_l, ks_l, vs_l, ss_l = [], [], [], [], [], []
    for l in range(DEPTH):
        w = (w_ada[l], b_ada[l], g_pre_mix[l], w_in[l], b_sb[l], w_gate_up[l], b_gate[l], g_sb_out[l],
             g_gla_out[l], w_out[l], g_post_mix[l], g_pre_ffn[l], w_ffn_gate[l], w_ffn_up[l],
             w_ffn_down[l], g_post_ffn[l])
        yp, kp, vp, sp = decoder_layer(yp, c_prompt, *w, None, None, None)
        k_past = cache_k[l][page_table].reshape(dec_b, -1, SB_HEADS, SB_HEAD_DIM)
        v_past = cache_v[l][page_table].reshape(dec_b, -1, SB_HEADS, SB_HEAD_DIM)
        ys, ks_, vs_, ss = decoder_layer(ys, c_sample, *w, k_past, v_past, state_gla[l])
        kp_l.append(kp); vp_l.append(vp); sp_l.append(sp)
        ks_l.append(ks_); vs_l.append(vs_); ss_l.append(ss)
    return (yp, ys, jnp.stack(kp_l), jnp.stack(vp_l), jnp.stack(sp_l),
            jnp.stack(ks_l), jnp.stack(vs_l), jnp.stack(ss_l))


_drawn_inputs = setup_inputs


def setup_inputs(seed=0):
    import zlib

    import numpy as np

    out = dict(_drawn_inputs(seed))
    spreads = {}
    factors = {'b_sb': 8.0,
     'g_sb_out': 4.629,
     'g_gla_out': 7.256,
     'g_post_mix': 3.77,
     'g_pre_ffn': 3.0,
     'g_post_ffn': 4.045}
    for name, (base, spread) in spreads.items():
        noise = np.random.default_rng([zlib.crc32(name.encode()), seed]).standard_normal(out[name].shape)
        drawn = base * np.exp(spread * noise) if base else spread * noise
        out[name] = __import__('jax').numpy.asarray(drawn.astype(out[name].dtype))
    for name, factor in factors.items():
        out[name] = (out[name] * factor).astype(out[name].dtype)
    return out
```

```python
from contextlib import ExitStack

import concourse.bass as bass
from concourse import mybir

F32 = mybir.dt.float32
F32R = mybir.dt.float32r
I32 = mybir.dt.int32
ACT = mybir.ActivationFunctionType
ALU = mybir.AluOpType
AX = mybir.AxisListType

P = 128
EPS = 1e-6
BIG = 30000.0


def stickbreak_gla_layer(nc, x_prompt, x_sample, c_prompt, c_sample, cache_k, cache_v, page_table, state_gla,
                         w_ada, b_ada, g_pre_mix, w_in, b_sb, w_gate_up, b_gate, g_sb_out, g_gla_out, w_out,
                         g_post_mix, g_pre_ffn, w_ffn_gate, w_ffn_up, w_ffn_down, g_post_ffn,
                         y_prompt, y_sample, new_k_prompt, new_v_prompt, new_state_prompt,
                         new_k_sample, new_v_sample, new_state_sample):
    D = x_prompt.shape[2]
    TP = x_prompt.shape[1]
    TS = x_sample.shape[0]
    T = TP + TS
    TB = TP // P
    KC = D // P
    H = b_sb.shape[1]
    DH = g_sb_out.shape[1]
    GH, DK, DV = state_gla.shape[2:]
    RANK = w_gate_up.shape[1]
    NPOOL = cache_k.shape[1]
    PAGES = page_table.shape[1]
    FF = w_ffn_gate.shape[2]
    FC = FF // P
    NMOD = w_ada.shape[2] // P
    NC = 1 + TS
    CG = 512
    MT = CG // P
    NIN = (w_in.shape[2] - RANK) // CG
    NOUT = D // CG
    NFF = FF // CG
    UPC = KC // 2
    NMA = 2 * D // CG
    HS = H * DH
    C_Q, C_K, C_V = 0, H, 2 * H
    C_GQ, C_GK, C_GV = 3 * H, 3 * H + GH, 3 * H + 2 * GH
    C_GR = C_GV + GH * DV // P
    NPROJ = C_GR + GH * DV // P
    SB_SCALE = float(DH) ** -0.5
    GLA_SCALE = float(DK) ** -0.5
    SUB = 16
    NSUB = TP // SUB
    VD = DV // P
    assert (D, TP, TS, H, DH, GH, DK, DV, PAGES, KC) == (2048, 256, 8, 8, 128, 4, 128, 256, 8, 16)

    ctx = ExitStack()
    with ctx:
        def sem(name):
            return ctx.enter_context(nc.semaphore(name))

        base = -(-nc.sbuf_base // 64) * 64
        slab_words = (nc.sbuf_usable_end - base) // 4 // 16 * 16
        ctx.enter_context(nc.sbuf_tensor("slab", [P, slab_words], F32))
        top = base + slab_words * 4
        cursor = [base]

        def put(name, shape, dt=F32, at=None):
            size = 4
            for s in shape[1:]:
                size *= s
            size = -(-size // 32) * 32
            if at is None:
                at = cursor[0]
                cursor[0] += size
            assert at + size <= top, (name, at + size, top)
            return nc.alloc_sbuf_tensor_at(name, shape, dt, offset=at), at + size

        RAW, _ = put("raw", [P, 4, 1024])
        at_split = cursor[0]
        HI, _ = put("w_hi", [P, 4, 1024], F32R)
        LO, _ = put("w_lo", [P, 4, 1024], F32R)
        at_h = cursor[0]
        H_HI, _ = put("h_hi", [P, KC, T], F32R)
        at_hlo = cursor[0]
        H_LO, _ = put("h_lo", [P, KC, T], F32R)
        X, _ = put("x_t", [P, KC, T])
        MOD, _ = put("mod_t", [P, NMOD, NC])
        ident, _ = put("ident", [P, P])
        ones, _ = put("ones", [P, P])
        triu, _ = put("triu", [P, P])
        vec1, _ = put("vec1", [P, NMOD + KC])
        vec2, _ = put("vec2", [P, 56])
        scale_t, _ = put("scale_t", [P, KC, NC])
        rstd, _ = put("rstd", [P, T])
        rvar, _ = put("rvar", [P, T])
        sel_c, _ = put("sel_c", [P, NC])
        sel_h, _ = put("sel_h", [P, H])
        bias_h, _ = put("bias_h", [P, H])
        r0 = cursor[0]

        A_HI, e1 = put("act_hi", [P, FC, T], F32R, at=r0)
        A_LO, e1 = put("act_lo", [P, FC, T], F32R, at=e1)
        GLU, e1 = put("glu", [P, MT, T], at=e1)
        F_HI, _ = put("f_hi", [P, KC, T], at=at_h)
        F_LO, _ = put("f_lo", [P, KC, T], at=at_hlo)
        PG, _ = put("pages", [P, 8, 1024], at=at_h)
        PROJ, rc = put("proj_t", [P, NPROJ, T], at=r0)
        MIX = PROJ[:, 0:KC, :]
        MT_ = PROJ[:, KC:2 * KC, :]
        SQD = PROJ[:, 2 * KC:3 * KC, :]
        AD4, a1 = put("ada4", [P, 4, 2048], at=r0)
        XR, a1 = put("x_rows", [P, 2, D], at=a1)
        ADA, b1 = put("ada2", [P, 2, 2048], at=rc)
        MROW, b1 = put("mod_row", [P, CG], at=b1)
        XS, b1 = put("xs_rows", [TS, D], at=b1)
        CR, b1 = put("c_rows", [NC, D], at=b1)
        CR2, _ = put("c_rows2", [NC, D], at=rc)
        VR, b1 = put("vec_rows", [P, 2, P], at=b1)
        WG, b1 = put("w_glow", [P, KC, RANK], at=b1)
        WGH, b1 = put("w_glow_hi", [P, KC, RANK], F32R, at=b1)
        WGL, b1 = put("w_glow_lo", [P, KC, RANK], F32R, at=b1)
        GLOW, c0 = put("g_low", [RANK, T], at=top - 1088)
        WGU, c0 = put("w_gate_up_s", [RANK, GH * DK], at=top - 1088 - 2048)
        PT, c0 = put("page_t", [1, TS * PAGES], I32, at=top - 1088 - 2048 - 256)
        c_top = top - 1088 - 2048 - 256
        CTK, _ = put("c_t_keep", [P, KC, 32], at=c_top - 2048)
        c_top -= 2048

        VTOK, c1 = put("v_tok", [P, TB, HS], at=rc)
        VG, c1 = put("vg_tok", [P, TB, GH * DV], at=c1)
        QBC, c1q = put("q_bcast", [P, 2, HS], at=c1)
        ZD, c1q = put("z_dec", [P, TS, PAGES * H], at=c1q)
        ZS, c1q = put("z_stage", [P, PAGES * H], at=c1q)
        ZB, c1q = put("sb_z", [P, 384], at=c1q)
        SE, c1q = put("sb_e", [P, 384], at=c1q)
        SL, c1q = put("sb_l", [P, 384], at=c1q)
        SA, c1q = put("sb_a", [P, 384], at=c1q)
        SP, c1q = put("sb_sp", [P, 384], at=c1q)
        M01, c1q = put("mask01", [P, 384], at=c1q)
        MNEG, c1q = put("maskneg", [P, 384], at=c1q)
        assert c1q <= c_top, (c1q, c_top)
        KTOK, s1 = put("k_tok", [P, HS], at=at_split)
        QTOK, s1 = put("qs_tok", [TS, HS], at=s1)
        KST, s1 = put("ks_tok", [TS, HS], at=s1)
        VST, s1 = put("vs_tok", [TS, HS], at=s1)
        SELB, s1 = put("sel_b", [TS, TS, P], at=s1)
        assert s1 <= at_h
        KTOK2, s1 = put("k_tok2", [P, HS], at=s1)
        AD, g1 = put("a_dec", [P, TS, PAGES * H], at=c1)
        CB0, g1 = put("cum0", [P, GH, TP], at=g1)
        CB1, g1 = put("cum1", [P, GH, TP], at=g1)
        CAB, g1 = put("cum_abs", [P, GH, TP], at=g1)
        QT, g1 = put("gla_q", [P, GH, TP], at=g1)
        KD, g1 = put("gla_kd", [P, 2, GH * TP], at=g1)
        BX, g1 = put("cum_blk", [P, GH, NSUB + 1], at=g1)
        GATE, g1 = put("gate", [P, GH, T], at=g1)
        at_kd = c1 + 2048 + 4 * 4096
        GT, _ = put("gate_t", [P, GH, T], at=at_kd)
        MIXV = GATE
        MIXR, _ = put("mix_rstd", [P, 4, T], at=at_kd)
        assert g1 <= c_top, (g1, c_top)
        DZ, t1 = put("dec_zb", [P, TS * PAGES * H], at=c1 + 2048)
        DE, t1 = put("dec_e", [P, TS * PAGES * H], at=t1)
        DL, t1 = put("dec_l", [P, TS * PAGES * H], at=t1)
        DR, t1 = put("dec_r", [P, TS, PAGES, H], at=c1 + 2 * HS * 4 + TS * PAGES * H * 4 + 256)
        off_v = r0 + C_V * T * 4
        DOUT, dv1 = put("dec_out", [P, HS], at=off_v)
        BD, dv1 = put("blockdiag", [P, P], at=dv1)
        ZSEL, dv1 = put("zsel", [P, P + SUB], at=dv1)
        QS, dv1 = put("qs_scaled", [P, GH, TS], at=dv1)
        ALP, dv1 = put("alpha", [P, GH, TS], at=dv1)
        DIAG, _ = put("diag", [P, 2, GH * TP], at=r0 + C_K * T * 4)
        GE, _ = put("gate_e", [P, GH, T], at=r0 + C_K * T * 4)
        GL, _ = put("gate_l", [P, GH, T], at=r0 + (C_K + GH) * T * 4)
        assert dv1 <= off_v + 8 * T * 4
        SS, q1 = put("state_s", [P, 2, TS, DV], at=at_split)
        ATT, q1 = put("att", [P, GH, 3, P], at=q1)
        KGS, q1 = put("kgs_tok", [TS, GH * DK], at=q1)
        VGS, q1 = put("vgs_tok", [TS, GH * DV], at=q1)
        KM, q1 = put("kgs_masked", [TS, TS, DK], at=q1)
        assert q1 <= at_h, (q1, at_h)
        SFIN = KD[:, 0, :].rearrange("p (h v) -> p h v", h=GH)
        KFT = KD[:, 1, :]
        SIL = PROJ[:, C_V:C_V + H, :]
        YROW, yy = put("y_rows", [P, TB, D], at=r0)
        YS, yy = put("y_s_rows", [TS, D], at=yy)
        y_jobs = [(tb * P, P, lambda q, tb=tb: YROW[:, tb, q * 512:q * 512 + 512]) for tb in range(TB)]
        y_jobs.append((TP, TS, lambda q: YS[:, q * 512:q * 512 + 512]))

        ps = ctx.enter_context(nc.psum_tensor("ps", [P, 8, 512], F32))

        win_v = w_in[0].rearrange("(k p) n -> p k n", p=P)
        wout_v = w_out[0].rearrange("(k p) n -> p k n", p=P)
        wg_v = w_ffn_gate[0].rearrange("(k p) n -> p k n", p=P)
        wu_v = w_ffn_up[0].rearrange("(k p) n -> p k n", p=P)
        wd_v = w_ffn_down[0].rearrange("(k p) n -> p k n", p=P)
        ada_v = w_ada[0].rearrange("(k p) n -> p k n", p=P)
        pool_k = cache_k[0].rearrange("n p h d -> n p (h d)")
        pool_v = cache_v[0].rearrange("n p h d -> n p (h d)")

        c_in = sem("c_in")
        x_in = sem("x_in")
        vec_in = sem("vec_in")
        misc_in = sem("misc_in")
        raw_in = [sem(f"raw_in{s}") for s in range(4)]
        ad4_in = [sem(f"ad4_in{s}") for s in range(4)]
        ada_in = [sem(f"ada_in{s}") for s in range(2)]
        page_in = [sem(f"page_in{s}") for s in range(8)]
        state_in = [sem(f"state_in{s}") for s in range(2)]
        state_out = [sem(f"state_out{s}") for s in range(2)]
        consts = sem("consts")
        hi_ready = sem("hi_ready")
        lo_ready = sem("lo_ready")
        unit_used = sem("unit_used")
        bank_done = sem("bank_done")
        bank_out = sem("bank_out")
        ad4_used = sem("ad4_used")
        ada_used = sem("ada_used")
        modrow_a = sem("modrow_a")
        modrow_b = sem("modrow_b")
        modt_a = sem("modt_a")
        modt_b = sem("modt_b")
        mod_a = sem("mod_a")
        mod_b = sem("mod_b")
        act_own = sem("act_own")
        dve_own = sem("dve_own")
        pool_own = sem("pool_own")
        silu_c = sem("silu_c")
        tr_done = sem("tr_done")
        ct_ready = sem("ct_ready")
        x_act = sem("x_act")
        x_dve = sem("x_dve")
        vec_ready = sem("vec_ready")
        sq_ready = sem("sq_ready")
        sums_done = sem("sums_done")
        h_ready = sem("h_ready")
        h32_ready = sem("h32_ready")
        hhi_ready = sem("hhi_ready")
        glow_mm = sem("glow_mm")
        wg_split = sem("wg_split")
        glow_ready = sem("glow_ready")
        tok_tr = sem("tok_tr")
        tok_act = sem("tok_act")
        tok_dve = sem("tok_dve")
        kv_out = sem("kv_out")
        kv_outb = sem("kv_outb")
        qb_mm = sem("qb_mm")
        qb_ready = sem("qb_ready")
        page_used = sem("page_used")
        sb_z = sem("sb_z")
        sb_abs = sem("sb_abs")
        sb_ln = sem("sb_ln")
        sb_sp = sem("sb_sp")
        sb_tail = sem("sb_tail")
        sb_arg = sem("sb_arg")
        sb_a = sem("sb_a")
        sb_o = sem("sb_o")
        sb_out = sem("sb_out")
        dve_loop = sem("dve_loop")
        act_loop = sem("act_loop")
        d_abs = sem("d_abs")
        d_ln = sem("d_ln")
        d_sp = sem("d_sp")
        d_tail = sem("d_tail")
        d_arg = sem("d_arg")
        d_a = sem("d_a")
        v_done = sem("v_done")
        v_evac = sem("v_evac")
        v_sel = sem("v_sel")
        v_put = sem("v_put")
        g_mm = sem("g_mm")
        g_abs = sem("g_abs")
        g_ln = sem("g_ln")
        g_cum = sem("g_cum")
        g_eq = sem("g_eq")
        g_qt = sem("g_qt")
        g_kdiff = sem("g_kdiff")
        g_kexp = sem("g_kexp")
        g_kd = sem("g_kd")
        g_off = sem("g_off")
        g_offev = sem("g_offev")
        g_ddiff = sem("g_ddiff")
        g_dexp = sem("g_dexp")
        g_dprod = sem("g_dprod")
        g_diag = sem("g_diag")
        g_att = sem("g_att")
        g_o = sem("g_o")
        g_oev = sem("g_oev")
        g_kft = sem("g_kft")
        g_kftev = sem("g_kftev")
        g_st = sem("g_st")
        g_stev = sem("g_stev")
        g_stout = sem("g_stout")
        km_ready = sem("km_ready")
        skv = sem("skv")
        snew = sem("snew")
        s_o = sem("s_o")
        s_oev = sem("s_oev")
        alp_ready = sem("alp_ready")
        var_ready = sem("var_ready")
        rs_ready = sem("rs_ready")
        msq = sem("msq")
        msum = sem("msum")
        r_exp = sem("r_exp")
        glu_e = sem("glu_e")
        glu_step = sem("glu_step")
        glu_hi = sem("glu_hi")
        glu_done = sem("glu_done")
        y_tr = sem("y_tr")
        y_act = sem("y_act")
        y_dve = sem("y_dve")
        y_out = sem("y_out")
        x_new = sem("x_new")

        W_OUT = NIN * UPC
        W_FFN = W_OUT + NOUT * UPC
        W_DOWN = W_FFN + 2 * NFF * UPC

        V_GPRE = NMOD
        V2 = dict(post_mix=0, pre_ffn=KC, post_ffn=2 * KC, b_gate=3 * KC, sb=3 * KC + GH, gla=3 * KC + GH + 1)
        NV2 = V2["gla"] + VD

        def linker(eng, own):
            n = [0]

            def link(ins):
                n[0] += 1
                ins.then_inc(own, 1)
                eng.wait_ge(own, n[0])
            return link

        tok_jobs = []
        for half in range(2):
            tok_jobs.append(([C_Q + 4 * half + j for j in range(4)], TP, TS, QTOK[:, half * 512:half * 512 + 512]))
        for tb in range(TB):
            for half in range(2):
                dst = (KTOK, KTOK2)[tb]
                tok_jobs.append(([C_K + 4 * half + j for j in range(4)], tb * P, P, dst[:, half * 512:half * 512 + 512]))
            for half in range(2):
                tok_jobs.append(([C_V + 4 * half + j for j in range(4)], tb * P, P,
                                 VTOK[:, tb, half * 512:half * 512 + 512]))
            for half in range(2):
                tok_jobs.append(([C_GV + 4 * half + j for j in range(4)], tb * P, P,
                                 VG[:, tb, half * 512:half * 512 + 512]))
        for first, dst in ((C_K, KST), (C_V, VST)):
            for half in range(2):
                tok_jobs.append(([first + 4 * half + j for j in range(4)], TP, TS, dst[:, half * 512:half * 512 + 512]))
        NTOK = len(tok_jobs)
        tok2_jobs = [([C_GK + j for j in range(4)], TP, TS, KGS[:, 0:512])]
        for half in range(2):
            tok2_jobs.append(([C_GV + 4 * half + j for j in range(4)], TP, TS, VGS[:, half * 512:half * 512 + 512]))

        V_TICK = {2 + 4 * b: b for b in range(TS)}

        def dec_out(dve, v, h):
            dve.wait_ge(s_o, h + 1)
            v.tensor_copy(PROJ[:, KC // 2 + VD * h:KC // 2 + VD * h + VD, TP:T],
                          ps[:, 7, 0:VD * TS].rearrange("p (v b) -> p v b", v=VD)).then_inc(s_oev, 1)

        def kview(i):
            return KD[:, i % 2, 0:GH * SUB * i].rearrange("p (h n) -> p h n", h=GH)

        def dview(t):
            return DIAG[:, t % 2, 0:GH * NSUB * (SUB - t)].rearrange("p (b n) -> p b n", n=SUB - t)

        block = ctx.enter_context(nc.Block())

        @block.sync
        def _(sp):
            sp.dma_start(CR[0:1, :], c_prompt).then_inc(c_in, 16)
            sp.dma_start(CR[1:NC, :], c_sample).then_inc(c_in, 16)
            for tb in range(TB):
                sp.dma_start(XR[:, tb, :], x_prompt[0, tb * P:(tb + 1) * P, :]).then_inc(x_in, 16)
            sp.dma_start(XS[:, :], x_sample.rearrange("b o d -> (b o) d")).then_inc(x_in, 16)

            def ada_unit(g, a):
                return ada_v[:, 4 * a:4 * a + 4, bass.ds(g * CG, CG)]

            def dst4(t):
                return t.rearrange("p (k n) -> p k n", k=4)

            for a in range(4):
                sp.dma_start(dst4(AD4[:, a, :]), ada_unit(0, a)).then_inc(ad4_in[a], 16)
                if a == 0:
                    sp.dma_start(VR[0:NMOD, 0, :], b_ada.rearrange("o (k p) -> (o k) p", p=P)).then_inc(vec_in, 16)
                    sp.dma_start(VR[NMOD:NMOD + KC, 0, :],
                                 g_pre_mix.rearrange("o (k p) -> (o k) p", p=P)).then_inc(vec_in, 16)
                    for nme, t, n in (("post_mix", g_post_mix, KC), ("pre_ffn", g_pre_ffn, KC),
                                      ("post_ffn", g_post_ffn, KC), ("b_gate", b_gate, GH), ("sb", g_sb_out, 1),
                                      ("gla", g_gla_out, VD)):
                        sp.dma_start(VR[V2[nme]:V2[nme] + n, 1, :],
                                     t.rearrange("o (k p) -> (o k) p", p=P)).then_inc(vec_in, 16)
            sp.dma_start(bias_h[:, :], b_sb[0].partition_broadcast(P)).then_inc(misc_in, 16)
            sp.dma_start(WGU[:, :], w_gate_up[0]).then_inc(misc_in, 16)
            sp.dma_start(PT[:, :], page_table.rearrange("b n -> (b n)").unsqueeze(0)).then_inc(misc_in, 16)
            sp.dma_start(WG[:, :, :], win_v[:, :, NIN * CG:NIN * CG + RANK]).then_inc(misc_in, 16)
            with sp.Fori(1, NMA) as g:
                for a in range(4):
                    sp.wait_ge(ad4_used, g * 4 + (a - 3))
                    sp.dma_start(dst4(AD4[:, a, :]), ada_unit(g, a)).then_inc(ad4_in[a], 16)

            def w_dst(s):
                return RAW[:, s, :].rearrange("p (k n) -> p k n", k=2)

            def w_unit(view, g, u, n):
                s = u % 4
                if n is not None:
                    sp.wait_ge(lo_ready, n)
                sp.dma_start(w_dst(s), view[:, 2 * u:2 * u + 2, bass.ds(g * CG, CG)]).then_inc(raw_in[s], 16)

            for u in range(4):
                w_unit(win_v, 0, u, None)
            sp.wait_ge(ct_ready, 1)
            for u in range(UPC):
                if u >= 4:
                    w_unit(win_v, 0, u, u - 3)
                if u % 2:
                    a = u // 2
                    if a >= 2:
                        sp.wait_ge(ada_used, a - 1)
                    sp.dma_start(dst4(ADA[:, a % 2, :]), ada_unit(NMA, a)).then_inc(ada_in[a % 2], 16)
            with sp.Fori(1, NIN) as g:
                for u in range(UPC):
                    w_unit(win_v, g, u, g * UPC + (u - 3))
                    if u % 2:
                        a = u // 2
                        sp.wait_ge(ada_used, g * 4 + (a - 1))
                        sp.dma_start(dst4(ADA[:, a % 2, :]), ada_unit(g + NMA, a)).then_inc(ada_in[a % 2], 16)

            def pages(pool, b, first):
                for j in range(PAGES):
                    page = sp.value_load(PT[0:1, bass.ds(b * PAGES + j, 1)], min_val=0, max_val=NPOOL - 1)
                    if not first:
                        sp.wait_ge(page_used, b * PAGES + (j - PAGES + 1) if pool is pool_k else
                                   b * PAGES + (j - PAGES + 1 + TS * PAGES))
                    sp.dma_start(PG[:, j, :], pool[bass.ds(page, 1), :, :].rearrange("o p n -> p (o n)"))\
                        .then_inc(page_in[j], 16)

            sp.wait_ge(misc_in, 64)
            sp.wait_ge(glow_mm, 1)
            pages(pool_k, 0, True)
            with sp.Fori(1, TS) as b:
                pages(pool_k, b, False)
            with sp.Fori(0, TS) as b:
                pages(pool_v, b, False)
            for u in range(4):
                w_unit(wout_v, 0, u, W_OUT + u - 3)
            sp.wait_ge(kv_outb, 16 * TB)
            sp.wait_ge(v_put, TS)
            sp.wait_ge(g_oev, GH)
            sp.wait_ge(s_oev, GH)
            sp.wait_ge(g_stout, 16)
            for u in range(UPC):
                if u >= 4:
                    w_unit(wout_v, 0, u, W_OUT + u - 3)
                if u % 2:
                    a = u // 2
                    sp.wait_ge(ada_used, NIN * 4 + a - 1)
                    sp.dma_start(dst4(ADA[:, a % 2, :]), ada_unit(NMA + NIN, a)).then_inc(ada_in[a % 2], 16)
            with sp.Fori(1, NOUT) as g:
                for u in range(UPC):
                    w_unit(wout_v, g, u, g * UPC + (W_OUT + u - 3))
                    if u % 2:
                        a = u // 2
                        sp.wait_ge(ada_used, g * 4 + (NIN * 4 + a - 1))
                        sp.dma_start(dst4(ADA[:, a % 2, :]), ada_unit(g + (NMA + NIN), a)).then_inc(ada_in[a % 2], 16)
            with sp.Fori(0, NFF) as g:
                for u in range(UPC):
                    w_unit(wg_v, g, u, g * 2 * UPC + (W_FFN + u - 3))
                for u in range(UPC):
                    w_unit(wu_v, g, u, g * 2 * UPC + (W_FFN + UPC + u - 3))
            for half in range(2):
                with sp.Fori(0, FC // 4) as j:
                    for u in range(4):
                        sp.wait_ge(lo_ready, j * 4 + (W_DOWN + half * FC + u - 3))
                        sp.dma_start(RAW[:, u, :].unsqueeze(1), wd_v[:, bass.ds(j * 4 + u, 1), half * 1024:half * 1024 + 1024])\
                            .then_inc(raw_in[u], 16)

        @block.gpsimd
        def _(pool):
            link = linker(pool, pool_own)
            g = nc.gpsimd
            link(g.memset(ident[:, :], 0.0))
            link(g.affine_select(out=ident[:, :], in_=ident[:, :], compare_op=ALU.not_equal, fill=1.0, base=0,
                                 pattern=[[-1, P]], channel_multiplier=1))
            link(g.memset(ones[:, :], 1.0))
            link(g.memset(sel_c[:, :], 0.0))
            for j in range(4):
                ins = g.affine_select(out=sel_c[:, :], in_=sel_c[:, :], compare_op=ALU.not_equal, fill=1.0,
                                      base=-32 * j, pattern=[[-1, NC]], channel_multiplier=1)
                if j < 3:
                    link(ins)
                else:
                    ins.then_inc(consts, 1)
            link(g.affine_select(out=triu[:, :], in_=ones[:, :], compare_op=ALU.is_ge, fill=0.0, base=0,
                                 pattern=[[-1, P]], channel_multiplier=1))
            link(g.memset(sel_h[:, :], 0.0))
            for j in range(4):
                ins = g.affine_select(out=sel_h[:, :], in_=sel_h[:, :], compare_op=ALU.not_equal, fill=1.0,
                                      base=-40 * j, pattern=[[-1, H]], channel_multiplier=1)
                if j < 3:
                    link(ins)
                else:
                    ins.then_inc(consts, 1)
            pool.wait_ge(unit_used, W_OUT)
            pool.wait_ge(glow_mm, 1)
            pool.wait_ge(mod_b, NIN)
            link(g.memset(M01[:, :], 1.0))
            for c in (0, 256):
                ins = g.affine_select(out=M01[:, c:c + P], in_=M01[:, c:c + P], compare_op=ALU.is_gt, fill=0.0,
                                      base=0, pattern=[[1, P]], channel_multiplier=-1)
                link(ins)
            link(g.tensor_scalar(MNEG[:, :], M01[:, :], BIG, -BIG, ALU.mult, ALU.add))
            link(g.memset(SELB[:, :, :], 0.0))
            g.affine_select(out=SELB[:, :, :], in_=SELB[:, :, :], compare_op=ALU.not_equal, fill=1.0, base=0,
                            pattern=[[-1, TS], [0, P]], channel_multiplier=1).then_inc(consts, 1)
            pool.wait_ge(tok_act, NTOK // 2)
            pool.wait_ge(tok_dve, NTOK // 2)
            for tb in range(TB):
                rows = slice(tb * P, (tb + 1) * P)
                pool.dma_start(new_k_prompt[0, 0].rearrange("t h d -> t (h d)")[rows, :],
                               (KTOK, KTOK2)[tb][:, :]).then_inc(kv_out, 16)
                pool.dma_start(new_v_prompt[0, 0].rearrange("t h d -> t (h d)")[rows, :],
                               VTOK[:, tb, :]).then_inc(kv_outb, 16)
            pool.dma_start(new_k_sample[0].rearrange("b o h d -> (b o) (h d)"), KST[:, :]).then_inc(kv_out, 16)
            pool.dma_start(new_v_sample[0].rearrange("b o h d -> (b o) (h d)"), VST[:, :]).then_inc(kv_out, 16)
            pool.wait_ge(sb_out, H)
            pool.wait_ge(tok_tr, NTOK)
            link(g.memset(BD[:, :], GLA_SCALE))
            bd3 = BD[:, :].rearrange("p (a b) -> p a b", b=SUB)
            link(g.affine_select(out=bd3, in_=bd3, compare_op=ALU.is_ge, fill=0.0, base=0,
                                 pattern=[[-SUB, P // SUB], [0, SUB]], channel_multiplier=1))
            link(g.affine_select(out=bd3, in_=bd3, compare_op=ALU.is_ge, fill=0.0, base=SUB - 1,
                                 pattern=[[SUB, P // SUB], [0, SUB]], channel_multiplier=-1))
            link(g.memset(ZSEL[:, :], 0.0))
            g.memset(ZSEL[:, :].rearrange("p (a b) -> p a b", b=SUB)[:, :, SUB - 1:SUB], 1.0).then_inc(consts, 1)
            def state_load(h):
                pool.dma_start(SS[:, h % 2, :, :], state_gla[0, :, h].rearrange("b k v -> k b v"))\
                    .then_inc(state_in[h % 2], 16)
            pool.wait_ge(kv_out, 16 * 4)
            pool.wait_ge(qb_mm, TS)
            state_load(0)
            state_load(1)
            pool.wait_ge(tok_act, NTOK // 2 + 2)
            pool.wait_ge(tok_dve, NTOK // 2 + 1)
            for h in range(GH):
                if h >= 1:
                    pool.wait_ge(skv, h * (TS // 2))
                g.tensor_tensor(KM[:, :, :], KGS[:, h * DK:(h + 1) * DK].unsqueeze(1).to_broadcast([TS, TS, DK]),
                                ident[0:TS, 0:TS].unsqueeze(2).to_broadcast([TS, TS, DK]), ALU.mult)\
                    .then_inc(km_ready, 1)
                pool.wait_ge(snew, TS * (h + 1))
                pool.dma_start(new_state_sample[0, :, h].rearrange("b k v -> k b v"), SS[:, h % 2, :, :])\
                    .then_inc(state_out[h % 2], 16)
                if h + 2 < GH:
                    pool.wait_ge(state_out[h % 2], 16)
                    pool.wait_ge(s_o, h + 1)
                    state_load(h + 2)
            pool.wait_ge(g_stev, 2)
            pool.dma_start(new_state_prompt[0, 0].rearrange("h k v -> k h v"), SFIN).then_inc(g_stout, 16)
            pool.wait_ge(kv_outb, 16 * TB)
            pool.wait_ge(kv_out, 16 * (TB + 2))
            pool.wait_ge(g_stout, 16)
            for s in range(2):
                pool.wait_ge(state_out[s], 32)
            for tb in range(TB):
                pool.wait_ge(y_act, 2 * (tb + 1))
                pool.wait_ge(y_dve, 2 * (tb + 1))
                pool.dma_start(y_prompt[0, tb * P:(tb + 1) * P, :],
                               YROW[:, tb, :]).then_inc(y_out, 16)
            pool.wait_ge(y_act, 2 * (TB + 1))
            pool.wait_ge(y_dve, 2 * (TB + 1))
            pool.dma_start(y_sample.rearrange("b o d -> (b o) d"), YS[:, :]).then_inc(y_out, 16)
            pool.wait_ge(y_out, 16 * (TB + 1))

        @block.scalar
        def _(act):
            link = linker(act, act_own)
            s = nc.scalar
            act.wait_ge(c_in, 32)
            s.activation(CR2[:, :], CR[:, :], ACT.Exp, scale=-1.0).then_inc(silu_c, 1)
            for k in range(0, KC, 2):
                act.wait_ge(tr_done, 3 + k)
                s.activation(X[:, k, :], ps[:, k % 4, 0:T], ACT.Copy).then_inc(x_act, 1)

            def rs(dst, var, n):
                act.wait_ge(var_ready, n)
                link(s.activation(dst, var, ACT.Ln))
                s.activation(dst, dst, ACT.Exp, scale=-0.5).then_inc(rs_ready, 1)

            rs(rstd[:, :], rvar[:, :], 1)

            def mod_row(done, count, ready):
                act.wait_ge(done, count)
                s.activation(MROW[:, :], ps[:, 4, :], ACT.Copy).then_inc(ready, 1)

            with act.Fori(0, NMA) as g:
                mod_row(ad4_used, g * 4 + 4, modrow_a)

            def h_high(n0, before=None):
                for q in range(4):
                    if before is not None:
                        before(q)
                    act.wait_ge(h32_ready, n0 + q + 1)
                    s.activation(H_HI[:, 4 * q:4 * q + 4, :], F_LO[:, 4 * q:4 * q + 4, :], ACT.Copy)\
                        .then_inc(hhi_ready, 1)

            def hi(n, j, first=False):
                act.wait_ge(raw_in[j], n[0])
                if not first:
                    act.wait_ge(unit_used, n[1])
                s.activation(HI[:, j, :], RAW[:, j, :], ACT.Copy).then_inc(hi_ready, 1)

            def hi_n(nb, u, first=False):
                hi((nb * 4 + (64 // 4 * (u // 4) + 16), nb + (u - 3)), u % 4, first)

            def evac(dst, m, wait_val, used_val):
                if m < 3:
                    act.wait_ge(bank_done, wait_val)
                else:
                    act.wait_ge(unit_used, used_val)
                s.activation(dst, ps[:, m, 0:T], ACT.Copy).then_inc(bank_out, 1)

            for u in range(4):
                hi((16, 0), u, True)
            h_high(0)
            for u in range(4, 8):
                hi_n(0, u)
            act.wait_ge(misc_in, 64)
            s.activation(WGH[:, :, :], WG[:, :, :], ACT.Copy).then_inc(wg_split, 1)

            def group(g, w0, bank0, dst0, adag, last=False):
                for u in range(3):
                    hi_n(g * UPC + w0, u)
                for m in range(MT):
                    evac(PROJ[:, bass.ds(g * MT + (dst0 - MT + m), 1), :].rearrange("p o t -> p (o t)"), m,
                         g * 3 + (bank0 - 3 + m + 1), g * UPC + w0)
                mod_row(ada_used, g * 4 + adag, modrow_b)
                for u in range(3, UPC):
                    hi_n(g * UPC + w0, u)

            with act.Fori(1, NIN) as g:
                group(g, 0, 0, 0, 0)
            for m in range(MT):
                evac(PROJ[:, (NIN - 1) * MT + m, :], m, NIN * 3 - 3 + m + 1, NIN * UPC)
            mod_row(ada_used, NIN * 4, modrow_b)
            act.wait_ge(glow_mm, 1)
            s.activation(GLOW[:, :], ps[0:RANK, 6, 0:T], ACT.Copy).then_inc(glow_ready, 1)

            act.wait_ge(consts, 3)
            for j, (chunks, t0, nt, dst) in enumerate(tok_jobs):
                if j % 2 == 0:
                    act.wait_ge(tok_tr, j + 1)
                    s.activation(dst, ps[0:nt, j % 4, :], ACT.Copy).then_inc(tok_act, 1)
            def q_out(b, half, n, nused):
                act.wait_ge(qb_mm, n)
                if nused is not None:
                    act.wait_ge(page_used, nused)
                last = s.activation(QBC[:, half, 0:512], ps[:, 4, :], ACT.Copy)
                last = s.activation(QBC[:, half, 512:1024], ps[:, 5, :], ACT.Copy)
                last.then_inc(qb_ready, 1)

            q_out(0, 0, 1, None)
            q_out(1, 1, 2, None)
            for h in range(H):
                act.wait_ge(sb_abs, h + 1)
                s.activation(SE[:, :], SA[:, :], ACT.Exp, scale=-1.0).then_inc(act_loop, 1)
                act.wait_ge(act_loop, h + 1)
                s.activation(SL[:, :], SE[:, :], ACT.Ln, bias=1.0).then_inc(sb_ln, 1)
                act.wait_ge(sb_arg, h + 1)
                s.activation(SA[:, :], SA[:, :], ACT.Exp).then_inc(sb_a, 1)
                act.wait_ge(sb_o, h + 1)
                s.activation(PROJ[:, C_Q + h, 0:TP], ps[:, 2, 0:TP], ACT.Copy).then_inc(sb_out, 1)
                if h + 2 < TS:
                    q_out(h + 2, h % 2, h + 3, PAGES * (h + 1))
            act.wait_ge(d_abs, 1)
            link(s.activation(DE[:, :], DL[:, :], ACT.Exp, scale=-1.0))
            s.activation(DL[:, :], DE[:, :], ACT.Ln, bias=1.0).then_inc(d_ln, 1)
            act.wait_ge(d_arg, 1)
            s.activation(AD[:, :, :].rearrange("p b n -> p (b n)"), DE[:, :], ACT.Exp).then_inc(d_a, 1)
            for j in (NTOK, NTOK + 2):
                chunks, t0, nt, dst = tok2_jobs[j - NTOK]
                act.wait_ge(kv_out, 16 * (TB + 2))
                act.wait_ge(tok_tr, j + 1)
                s.activation(dst, ps[0:nt, j % 4, :], ACT.Copy).then_inc(tok_act, 1)

            def v_out(b):
                act.wait_ge(v_done, b + 1)
                if b >= 1:
                    act.wait_ge(v_sel, b)
                s.activation(DOUT[:, 0:512], ps[:, 4, :], ACT.Copy)
                s.activation(DOUT[:, 512:1024], ps[:, 5, :], ACT.Copy).then_inc(v_evac, 1)

            act.wait_ge(g_abs, 1)
            link(s.activation(GE[:, :, :], GL[:, :, :], ACT.Exp, scale=-1.0))
            s.activation(GL[:, :, :], GE[:, :, :], ACT.Ln, bias=1.0).then_inc(g_ln, 1)
            act.wait_ge(g_cum, 1)
            s.activation(ALP[:, :, :], GATE[:, :, TP:T], ACT.Exp, scale=-1.0 / 16).then_inc(alp_ready, 1)
            s.activation(QT[:, :, :], CB1[:, :, :], ACT.Exp, scale=-1.0 / 16).then_inc(g_eq, 1)
            for i in range(1, NSUB + 1):
                act.wait_ge(g_kdiff, i)
                s.activation(kview(i), kview(i), ACT.Exp, scale=1.0 / 16).then_inc(g_kexp, 1)
                if i - 3 in V_TICK:
                    v_out(V_TICK[i - 3])
            for t in range(SUB):
                act.wait_ge(g_ddiff, t + 1)
                s.activation(dview(t), dview(t), ACT.Exp, scale=-1.0 / 16).then_inc(g_dexp, 1)
                if t < 2:
                    act.wait_ge(g_kft, t + 1)
                    s.activation(KFT[:, t * 512:t * 512 + 512], ps[:, 2 + t, :], ACT.Copy).then_inc(g_kftev, 1)
                elif t < 4:
                    act.wait_ge(g_st, t - 1)
                    s.activation(SFIN[:, 2 * (t - 2):2 * (t - 2) + 2, :].rearrange("p h v -> p (h v)"),
                                 ps[:, t, :], ACT.Copy).then_inc(g_stev, 1)
                if NSUB + t - 2 in V_TICK:
                    v_out(V_TICK[NSUB + t - 2])
            for h in range(GH):
                act.wait_ge(g_o, h + 1)
                s.activation(PROJ[:, KC // 2 + VD * h:KC // 2 + VD * h + VD, 0:TP],
                             ps[:, 2 + h % 2, :].rearrange("p (v t) -> p v t", v=VD), ACT.Copy).then_inc(g_oev, 1)
            v_out(TS - 1)
            act.wait_ge(v_sel, TS)
            act.wait_ge(s_o, GH)
            s.activation(SIL, PROJ[:, C_GR:C_GR + 8, :], ACT.Exp, scale=-1.0).then_inc(r_exp, 1)

            for st in range(2):
                act.wait_ge(state_out[st], 32)
            act.wait_ge(g_stout, 16)
            for u in range(4):
                hi_n(W_OUT, u)

            def mix_rs(q):
                nb = 4 if q < 2 else 2
                rs(MIXR[:, 0:nb, :], MIXV[:, 0:nb, :], 2 + q)

            h_high(4, mix_rs)
            for u in range(4, 8):
                hi_n(W_OUT, u)
            B1 = NIN * 3
            with act.Fori(1, NOUT) as g:
                group(g, W_OUT, B1, KC, NIN * 4)
            for m in range(MT):
                evac(PROJ[:, KC + (NOUT - 1) * MT + m, :], m, B1 + NOUT * 3 - 3 + m + 1, W_OUT + NOUT * UPC)
            mod_row(ada_used, (NIN + NOUT) * 4, modrow_b)
            rs(rstd[:, :], rvar[:, :], 6)
            rs(rstd[:, :], rvar[:, :], 7)

            def glu_exp(g):
                act.wait_ge(unit_used, g * 2 * UPC + (W_FFN + UPC))
                s.activation(GLU[:, :, :], ps[:, 0:MT, 0:T], ACT.Exp, scale=-1.0).then_inc(glu_e, 1)

            def glu_high(g):
                act.wait_ge(glu_step, g * 4 + 4)
                s.activation(A_HI[:, bass.ds(g * MT, MT), :], GLU[:, :, :], ACT.Copy).then_inc(glu_hi, 1)

            def ffn(g, prev):
                for u in range(3):
                    hi_n(g * 2 * UPC + W_FFN, u)
                if prev is not None:
                    glu_high(prev)
                for u in range(3, UPC + 3):
                    hi_n(g * 2 * UPC + W_FFN, u)
                if prev is not None:
                    act.wait_ge(glu_done, prev + 1)
                glu_exp(g)
                for u in range(UPC + 3, 2 * UPC):
                    hi_n(g * 2 * UPC + W_FFN, u)

            for u in range(4):
                hi_n(W_FFN, u)
            h_high(8)
            for u in range(4, UPC + 3):
                hi_n(W_FFN, u)
            glu_exp(0)
            for u in range(UPC + 3, 2 * UPC):
                hi_n(W_FFN, u)
            with act.Fori(1, NFF) as g:
                ffn(g, g - 1)

            def down4(nb, mid=None):
                for u in range(4):
                    if u == 3 and mid:
                        mid()
                    hi_n(nb, u)

            down4(W_DOWN, lambda: glu_high(NFF - 1))
            with act.Fori(1, FC // 4) as j:
                down4(j * 4 + W_DOWN)
            BD0 = (NIN + NOUT) * 3

            def down_out(half):
                for m in range(8):
                    if m < 7:
                        act.wait_ge(bank_done, BD0 + half * 7 + m + 1)
                    else:
                        act.wait_ge(unit_used, W_DOWN + (half + 1) * FC)
                    s.activation(F_HI[:, half * 8 + m, :], ps[:, m, 0:T], ACT.Copy).then_inc(bank_out, 1)

            down4(W_DOWN + FC, lambda: down_out(0))
            with act.Fori(1, FC // 4) as j:
                down4(j * 4 + (W_DOWN + FC))
            down_out(1)
            rs(rstd[:, :], rvar[:, :], 8)

            n = 0
            for t0, nt, dst in y_jobs:
                for q in range(4):
                    if q % 2 == 0:
                        act.wait_ge(y_tr, n + 1)
                        s.activation(dst(q), ps[0:nt, 2 + n % 4, :], ACT.Copy).then_inc(y_act, 1)
                    n += 1


        @block.vector
        def _(dve):
            link = linker(dve, dve_own)
            v = nc.vector
            link(v.memset(CTK[:, :, :], 0.0))
            dve.wait_ge(silu_c, 1)
            link(v.tensor_scalar(CR2[:, :], CR2[:, :], 1.0, None, ALU.add))
            link(v.reciprocal(CR2[:, :], CR2[:, :]))
            v.tensor_tensor(CR[:, :], CR[:, :], CR2[:, :], ALU.mult).then_inc(silu_c, 1)
            dve.wait_ge(tr_done, 1)
            v.tensor_copy(CTK[:, :, 0:NC], ps[:, 7, 0:KC * NC].rearrange("p (k t) -> p k t", k=KC)).then_inc(ct_ready, 1)
            dve.wait_ge(tr_done, 2)
            v.tensor_copy(vec1[:, :], ps[:, 5, 0:NMOD + KC]).then_inc(vec_ready, 1)
            v.tensor_copy(vec2[:, 0:NV2], ps[:, 5, 128:128 + NV2]).then_inc(vec_ready, 1)
            for k in range(1, KC, 2):
                dve.wait_ge(tr_done, 3 + k)
                v.tensor_copy(X[:, k, :], ps[:, k % 4, 0:T]).then_inc(x_dve, 1)
            dve.wait_ge(x_act, KC // 2)
            dve.wait_ge(x_dve, KC // 2)
            for q in range(4):
                xq = X[:, 4 * q:4 * q + 4, :]
                v.tensor_tensor(F_LO[:, 4 * q:4 * q + 4, :], xq, xq, ALU.mult).then_inc(sq_ready, 1)

            def rstd_of(dst, var, src, width, n):
                v.tensor_scalar(var, src, 1.0 / width, EPS, ALU.mult, ALU.add).then_inc(var_ready, 1)
                dve.wait_ge(rs_ready, n)
                link(v.tensor_tensor(var, var, dst, ALU.mult))
                link(v.tensor_tensor(var, var, dst, ALU.mult))
                link(v.tensor_scalar(var, var, -0.5, 1.5, ALU.mult, ALU.add))
                link(v.tensor_tensor(dst, dst, var, ALU.mult))

            dve.wait_ge(sums_done, 1)
            rstd_of(rstd[:, :], rvar[:, :], ps[:, 6, 0:T], D, 1)
            dve.wait_ge(vec_ready, 2)

            def mod_col(made, count, g, ready):
                dve.wait_ge(made, count)
                v.tensor_tensor(MOD[:, bass.ds(g * 4, 4), :],
                                ps[:, 5, 0:4 * NC].rearrange("p (m t) -> p m t", m=4),
                                vec1[:, bass.ds(g * 4, 4)].unsqueeze(2).to_broadcast([P, 4, NC]), ALU.add)\
                    .then_inc(ready, 1)

            with dve.Fori(0, NMA) as g:
                mod_col(modt_a, g + 1, g, mod_a)

            def low_h(n0, q):
                cs = slice(4 * q, 4 * q + 4)
                dve.wait_ge(hhi_ready, n0 + q + 1)
                v.tensor_tensor(H_LO[:, cs, :], F_LO[:, cs, :], H_HI[:, cs, :].bitcast(F32), ALU.subtract)\
                    .then_inc(h_ready, 1)

            def build_h(gain, shift, scl, n0):
                link(v.scalar_tensor_tensor(scale_t[:, :, :], MOD[:, scl:scl + KC, :], 1.0,
                                            gain.unsqueeze(2).to_broadcast([P, KC, NC]), ALU.add, ALU.mult))
                for q in range(4):
                    cs = slice(4 * q, 4 * q + 4)
                    link(v.tensor_tensor(F_LO[:, cs, :], X[:, cs, :], rstd[:, :].unsqueeze(1).to_broadcast([P, 4, T]),
                                         ALU.mult))
                    link(v.tensor_tensor(F_LO[:, cs, TP:T], F_LO[:, cs, TP:T], scale_t[:, cs, 1:NC], ALU.mult))
                    v.tensor_tensor(F_LO[:, cs, TP:T], F_LO[:, cs, TP:T],
                                    MOD[:, shift + 4 * q:shift + 4 * q + 4, 1:NC], ALU.add)
                    for k in range(4 * q, 4 * q + 4):
                        ins = v.tensor_scalar(F_LO[:, k, 0:TP], F_LO[:, k, 0:TP], scale_t[:, k, 0:1],
                                              MOD[:, shift + k, 0:1], ALU.mult, ALU.add)
                    ins.then_inc(h32_ready, 1)
                    if q >= 1:
                        low_h(n0, q - 1)
                low_h(n0, 3)

            def lo(nb, u):
                dve.wait_ge(hi_ready, nb + (u + 1))
                v.tensor_tensor(LO[:, u % 4, :], RAW[:, u % 4, :], HI[:, u % 4, :].bitcast(F32), ALU.subtract)\
                    .then_inc(lo_ready, 1)

            dve.wait_ge(mod_a, NMA)
            for u in range(4):
                lo(0, u)
            build_h(vec1[:, NMOD:NMOD + KC], 0, KC, 0)
            for u in range(4, UPC):
                lo(0, u)
            dve.wait_ge(wg_split, 1)
            v.tensor_tensor(WGL[:, :, :], WG[:, :, :], WGH[:, :, :].bitcast(F32), ALU.subtract).then_inc(wg_split, 1)

            with dve.Fori(1, NIN) as g:
                for u in range(7):
                    lo(g * UPC, u)
                mod_col(modt_b, g, g + (NMA - 1), mod_b)
                lo(g * UPC, 7)
            mod_col(modt_b, NIN, NIN + NMA - 1, mod_b)

            dve.wait_ge(consts, 3)
            for j, (chunks, t0, nt, dst) in enumerate(tok_jobs):
                if j % 2:
                    dve.wait_ge(tok_tr, j + 1)
                    v.tensor_copy(dst, ps[0:nt, j % 4, :]).then_inc(tok_dve, 1)

            def softplus_tail(e, l, z, t, out, chain):
                chain(v.tensor_scalar(t, e, 1.0, None, ALU.add))
                chain(v.scalar_tensor_tensor(t, t, 1.0, e, ALU.subtract, ALU.subtract))
                chain(v.tensor_tensor(t, l, t, ALU.subtract))
                chain(v.scalar_tensor_tensor(out, z, 0.0, t, ALU.max, ALU.add))

            NSTEP = 7
            with dve.Fori(0, TS // 2) as b2:
                step = [0]

                def chain(ins):
                    step[0] += 1
                    ins.then_inc(dve_loop, 1)
                    dve.wait_ge(dve_loop, b2 * (2 * NSTEP) + step[0])

                for e in range(2):
                    def nth(k, per=1):
                        return b2 * (2 * per) + (e * per + k)

                    def dots(pg):
                        dve.wait_ge(page_in[pg], nth(1, 1) * 16)
                        for h in range(H):
                            kp = PG[:, pg, h * DH:(h + 1) * DH]
                            ins = v.tensor_tensor_reduce(kp, kp, QBC[:, e, h * DH:(h + 1) * DH], 1.0, 0.0,
                                                         ALU.mult, ALU.add, ZS[:, pg * H + h:pg * H + h + 1])
                        ins.then_inc(page_used, 1)

                    dve.wait_ge(qb_ready, nth(1))
                    dve.wait_ge(sb_z, nth(1))
                    chain(v.tensor_scalar(ZB[:, :], ps[:, 0, 0:384], SB_SCALE, bias_h[:, bass.ds(b2 * 2 + e, 1)],
                                          ALU.mult, ALU.add))
                    v.scalar_tensor_tensor(SA[:, :], ZB[:, :], -1.0, ZB[:, :], ALU.mult, ALU.max).then_inc(sb_abs, 1)
                    for pg in range(0, 3):
                        dots(pg)
                    dve.wait_ge(sb_ln, nth(1))
                    softplus_tail(SE[:, :], SL[:, :], ZB[:, :], SP[:, :], SP[:, :], chain)
                    v.tensor_tensor(SP[:, :], SP[:, :], M01[:, :], ALU.mult).then_inc(sb_sp, 1)
                    for pg in range(3, 6):
                        dots(pg)
                    dve.wait_ge(sb_tail, nth(1))
                    chain(v.tensor_tensor(SA[:, :], ZB[:, :], ps[:, 1, 0:384], ALU.subtract))
                    v.scalar_tensor_tensor(SA[:, :], SA[:, :], 0.0, MNEG[:, :], ALU.min, ALU.add).then_inc(sb_arg, 1)
                    for pg in range(6, 8):
                        dots(pg)
                    dve.wait_ge(page_used, nth(PAGES, PAGES))
                    chain(v.tensor_copy(ZD[:, bass.ds(b2 * 2 + e, 1), :].rearrange("p o n -> p (o n)"), ZS[:, :]))
                assert step[0] == 2 * NSTEP, step

            zd = ZD[:, :, :].rearrange("p b n -> p (b n)")
            dve.wait_ge(sb_a, H)
            link(v.scalar_tensor_tensor(DZ[:, :].rearrange("p (n h) -> p n h", h=H),
                                        zd.rearrange("p (n h) -> p n h", h=H), SB_SCALE,
                                        bias_h[:, :].unsqueeze(1).to_broadcast([P, TS * PAGES, H]), ALU.mult, ALU.add))
            v.scalar_tensor_tensor(DL[:, :], DZ[:, :], -1.0, DZ[:, :], ALU.mult, ALU.max).then_inc(d_abs, 1)
            dve.wait_ge(d_ln, 1)
            softplus_tail(DE[:, :], DL[:, :], DZ[:, :], zd, zd, link)
            zp = zd.rearrange("p (b g h) -> p b g h", b=TS, g=PAGES)
            link(v.memset(DR[:, :, PAGES - 1, :], 0.0))
            for pg in range(PAGES - 2, -1, -1):
                ins = v.tensor_tensor(DR[:, :, pg, :], DR[:, :, pg + 1, :], zp[:, :, pg + 1, :], ALU.add)
                if pg:
                    link(ins)
            ins.then_inc(d_sp, 1)
            dve.wait_ge(d_tail, 1)
            link(v.tensor_tensor(DE[:, :], DZ[:, :], ps[:, 1, :], ALU.subtract))
            v.tensor_scalar(DE[:, :], DE[:, :], 0.0, None, ALU.min).then_inc(d_arg, 1)
            dve.wait_ge(kv_out, 16 * (TB + 2))
            dve.wait_ge(tok_tr, NTOK + 2)
            v.tensor_copy(tok2_jobs[1][3], ps[0:TS, (NTOK + 1) % 4, :]).then_inc(tok_dve, 1)

            dve.wait_ge(d_a, 1)
            for h in range(GH):
                dve.wait_ge(g_mm, h + 1)
                link(v.tensor_scalar(GATE[:, h, :], ps[:, h, 0:T], vec2[:, V2["b_gate"] + h:V2["b_gate"] + h + 1], -1.0,
                                     ALU.add, ALU.mult))
            v.scalar_tensor_tensor(GL[:, :, :], GATE[:, :, :], -1.0, GATE[:, :, :], ALU.mult, ALU.max).then_inc(g_abs, 1)
            dve.wait_ge(g_ln, 1)
            softplus_tail(GE[:, :, :], GL[:, :, :], GATE[:, :, :], GT[:, :, :], GATE[:, :, :], link)
            def blocks(t):
                return t[:, :, 0:TP].rearrange("p h (b n) -> p h b n", n=SUB)
            src, dst = GATE, CB0
            for k in (1, 2, 4, 8):
                link(v.tensor_tensor(blocks(dst)[:, :, :, k:], blocks(src)[:, :, :, k:],
                                     blocks(src)[:, :, :, 0:SUB - k], ALU.add))
                link(v.tensor_copy(blocks(dst)[:, :, :, 0:k], blocks(src)[:, :, :, 0:k]))
                src, dst = dst, (CB1 if dst is CB0 else CB0)
            link(v.memset(BX[:, :, 0:1], 0.0))
            for i in range(NSUB):
                link(v.tensor_tensor(BX[:, :, i + 1:i + 2], BX[:, :, i:i + 1],
                                     CB1[:, :, i * SUB + SUB - 1:i * SUB + SUB], ALU.add))
            v.tensor_tensor(blocks(CAB), blocks(CB1), BX[:, :, 0:NSUB].unsqueeze(3).to_broadcast([P, GH, NSUB, SUB]),
                            ALU.add).then_inc(g_cum, 1)
            dve.wait_ge(tok_tr, NTOK + 3)
            dve.wait_ge(consts, 4)
            v.tensor_scalar(QS[:, :, :], PROJ[:, C_GQ:C_GQ + GH, TP:T], GLA_SCALE, None, ALU.mult).then_inc(alp_ready, 1)
            dve.wait_ge(g_eq, 1)
            v.scalar_tensor_tensor(QT[:, :, :], PROJ[:, C_GQ:C_GQ + GH, 0:TP], GLA_SCALE, QT[:, :, :],
                                   ALU.mult, ALU.mult).then_inc(g_qt, 1)
            for h in range(GH):
                v.memset(ps[:, h, 0:384], 0.0).then_inc(g_qt, 1)
            dve.wait_ge(g_cum, 1)

            def put_row(b):
                dve.wait_ge(v_sel, b + 1)
                v.tensor_copy(PROJ[:, 0:H, TP + b:TP + b + 1], ps[:, 6, 0:H].unsqueeze(2)).then_inc(v_put, 1)

            def kdiff(i):
                if i >= 3:
                    dve.wait_ge(g_off, i - 2)
                v.tensor_tensor(kview(i), CAB[:, :, 0:SUB * i], BX[:, :, i:i + 1].to_broadcast([P, GH, SUB * i]),
                                ALU.subtract).then_inc(g_kdiff, 1)

            kdiff(1)
            for i in range(1, NSUB + 1):
                if i < NSUB:
                    kdiff(i + 1)
                dve.wait_ge(g_kexp, i)
                v.tensor_tensor(kview(i), kview(i), PROJ[:, C_GK:C_GK + GH, 0:SUB * i], ALU.mult).then_inc(g_kd, 1)
                if i - 1 in V_TICK and V_TICK[i - 1] >= 1:
                    put_row(V_TICK[i - 1] - 1)
            dve.wait_ge(g_off, NSUB - 1)
            for h in range(GH):
                v.tensor_copy(ATT[:, h, :, :].rearrange("p a b -> p (a b)"), ps[:, h, 0:384]).then_inc(g_offev, 1)

            def in_blocks(c0, a, b):
                return PROJ[:, c0:c0 + GH, 0:TP].rearrange("p h (b n) -> p h b n", n=SUB)[:, :, :, a:b]

            def d4(t):
                return dview(t).rearrange("p (h b) n -> p h b n", h=GH)

            cb = CB1[:, :, :].rearrange("p h (b n) -> p (h b) n", n=SUB)

            def ddiff(t):
                if t >= 2:
                    dve.wait_ge(g_diag, t - 1)
                v.tensor_tensor(dview(t), cb[:, :, t:SUB], cb[:, :, t:t + 1].to_broadcast([P, GH * NSUB, SUB - t]),
                                ALU.subtract).then_inc(g_ddiff, 1)

            ddiff(0)
            for t in range(SUB):
                if t + 1 < SUB:
                    ddiff(t + 1)
                dve.wait_ge(g_dexp, t + 1)
                link(v.tensor_tensor(d4(t), d4(t), in_blocks(C_GQ, t, SUB), ALU.mult))
                v.tensor_tensor(d4(t), d4(t), in_blocks(C_GK, t, t + 1).to_broadcast([P, GH, NSUB, SUB - t]),
                                ALU.mult).then_inc(g_dprod, 1)
                if NSUB + t - 1 in V_TICK:
                    put_row(V_TICK[NSUB + t - 1] - 1)
            dve.wait_ge(g_diag, SUB)
            dve.wait_ge(g_offev, GH)
            diag_t = CAB[:, 0, :].rearrange("p (a b) -> p a b", a=2)
            for h in range(GH):
                link(v.tensor_tensor(diag_t, ps[:, h // 2, (h % 2) * TP:(h % 2) * TP + TP].rearrange("p (a b) -> p a b", a=2),
                                     BD[:, :].unsqueeze(1).to_broadcast([P, 2, P]), ALU.mult))
                v.tensor_tensor(ATT[:, h, 0:3:2, :], ATT[:, h, 0:3:2, :], diag_t, ALU.add).then_inc(g_att, 1)
                dve.wait_ge(g_att, h + 1)

            dve.wait_ge(alp_ready, 2)
            for h in range(GH):
                dve.wait_ge(state_in[h % 2], 16 * (h // 2 + 1))
                for b in range(TS):
                    if b % 2 == 0:
                        dve.wait_ge(skv, h * (TS // 2) + b // 2 + 1)
                    st = SS[:, h % 2, b, :]
                    v.scalar_tensor_tensor(st, st, ALP[:, h, b:b + 1], ps[:, b // 2, (b % 2) * DV:(b % 2) * DV + DV],
                                           ALU.mult, ALU.add).then_inc(snew, 1)
                if h >= 1:
                    dec_out(dve, v, h - 1)
            dec_out(dve, v, GH - 1)
            put_row(TS - 1)

            dve.wait_ge(r_exp, 1)
            link(v.tensor_scalar(SIL, SIL, 1.0, None, ALU.add))
            link(v.reciprocal(SIL, SIL))
            link(v.tensor_tensor(SIL, SIL, PROJ[:, C_GR:C_GR + 8, :], ALU.mult))
            dve.wait_ge(v_put, TS)
            dve.wait_ge(s_oev, GH)
            dve.wait_ge(g_oev, GH)
            dve.wait_ge(sb_out, H)
            for q in range(4):
                mq = MIX[:, 4 * q:4 * q + 4, :]
                v.tensor_tensor(F_LO[:, 4 * q:4 * q + 4, :], mq, mq, ALU.mult).then_inc(msq, 1)
            for u in range(4):
                lo(W_OUT, u)
            for q in range(4):
                dve.wait_ge(msum, q + 1)
                nb = 4 if q < 2 else 2
                rt = MIXR[:, 0:nb, :]
                b0 = 4 * (q % 2)
                rstd_of(rt, MIXV[:, 0:nb, :], ps[:, b0:b0 + nb, 0:T], DH if q < 2 else DV, 2 + q)
                if q < 2:
                    cs = slice(4 * q, 4 * q + 4)
                    v.scalar_tensor_tensor(F_LO[:, cs, :], MIX[:, cs, :], vec2[:, V2["sb"]:V2["sb"] + 1], rt,
                                           ALU.mult, ALU.mult).then_inc(h32_ready, 1)
                else:
                    for vb in range(VD):
                        cs = slice(4 * q + vb, 4 * q + vb + 3, 2)
                        link(v.scalar_tensor_tensor(F_LO[:, cs, :], MIX[:, cs, :],
                                                    vec2[:, V2["gla"] + vb:V2["gla"] + vb + 1], rt, ALU.mult, ALU.mult))
                    cs = slice(4 * q, 4 * q + 4)
                    v.tensor_tensor(F_LO[:, cs, :], F_LO[:, cs, :], SIL[:, 4 * (q - 2):4 * (q - 2) + 4, :],
                                    ALU.mult).then_inc(h32_ready, 1)
                low_h(4, q)
                dve.wait_ge(h_ready, 4 + q + 1)

            for u in range(4, UPC):
                lo(W_OUT, u)
            with dve.Fori(1, NOUT) as g:
                for u in range(7):
                    lo(g * UPC + W_OUT, u)
                mod_col(modt_b, g + NIN, g + (NMA + NIN - 1), mod_b)
                lo(g * UPC + W_OUT, 7)
            mod_col(modt_b, NIN + NOUT, NIN + NOUT + NMA - 1, mod_b)

            def add_norm(src, gain, gate, squares, done, n, nr, nx):
                dve.wait_ge(bank_out, n)
                for q in range(4):
                    sq = src[:, 4 * q:4 * q + 4, :]
                    v.tensor_tensor(squares[:, 4 * q:4 * q + 4, :], sq, sq, ALU.mult).then_inc(sq_ready, 1)
                link(v.tensor_tensor(scale_t[:, :, :], MOD[:, gate:gate + KC, :],
                                     gain.unsqueeze(2).to_broadcast([P, KC, NC]), ALU.mult))
                dve.wait_ge(sums_done, done)
                rstd_of(rstd[:, :], rvar[:, :], ps[:, 6, 0:T], D, nr)
                for q in range(4):
                    cs = slice(4 * q, 4 * q + 4)
                    link(v.tensor_tensor(src[:, cs, :], src[:, cs, :], rstd[:, :].unsqueeze(1).to_broadcast([P, 4, T]),
                                         ALU.mult))
                    link(v.tensor_tensor(squares[:, cs, TP:T], src[:, cs, TP:T], scale_t[:, cs, 1:NC], ALU.mult))
                    v.tensor_tensor(X[:, cs, TP:T], X[:, cs, TP:T], squares[:, cs, TP:T], ALU.add)
                    for k in range(4 * q, 4 * q + 4):
                        ins = v.scalar_tensor_tensor(X[:, k, 0:TP], src[:, k, 0:TP], scale_t[:, k, 0:1], X[:, k, 0:TP],
                                                     ALU.mult, ALU.add)
                    ins.then_inc(x_new, 1)
                    dve.wait_ge(x_new, nx + q + 1)
                    yield q

            dve.wait_ge(mod_b, NIN + NOUT)
            for q in add_norm(MT_, vec2[:, V2["post_mix"]:V2["post_mix"] + KC], 2 * KC, SQD, 2, 4 * (NIN + NOUT), 6, 0):
                xq = X[:, 4 * q:4 * q + 4, :]
                v.tensor_tensor(SQD[:, 4 * q:4 * q + 4, :], xq, xq, ALU.mult).then_inc(sq_ready, 1)
            dve.wait_ge(sums_done, 3)
            rstd_of(rstd[:, :], rvar[:, :], ps[:, 7, 0:T], D, 7)
            for u in range(4):
                lo(W_FFN, u)
            build_h(vec2[:, V2["pre_ffn"]:V2["pre_ffn"] + KC], 3 * KC, 4 * KC, 8)

            def glu_gate(g):
                dve.wait_ge(glu_e, g + 1)
                v.tensor_scalar(GLU[:, :, :], GLU[:, :, :], 1.0, None, ALU.add).then_inc(glu_step, 1)
                dve.wait_ge(glu_step, g * 4 + 1)
                v.reciprocal(GLU[:, :, :], GLU[:, :, :]).then_inc(glu_step, 1)
                dve.wait_ge(glu_step, g * 4 + 2)
                v.tensor_tensor(GLU[:, :, :], GLU[:, :, :], ps[:, 0:MT, 0:T], ALU.mult).then_inc(glu_step, 1)

            def glu_up(g):
                dve.wait_ge(unit_used, g * (2 * UPC) + (W_FFN + 2 * UPC))
                dve.wait_ge(glu_step, g * 4 + 3)
                v.tensor_tensor(GLU[:, :, :], GLU[:, :, :], ps[:, MT:2 * MT, 0:T], ALU.mult).then_inc(glu_step, 1)

            def glu_low(g):
                dve.wait_ge(glu_hi, g + 1)
                v.tensor_tensor(A_LO[:, bass.ds(g * MT, MT), :], GLU[:, :, :],
                                A_HI[:, bass.ds(g * MT, MT), :].bitcast(F32), ALU.subtract).then_inc(glu_done, 1)

            for u in range(4, UPC + 3):
                lo(W_FFN, u)
            glu_gate(0)
            for u in range(UPC + 3, 2 * UPC):
                lo(W_FFN, u)
            with dve.Fori(1, NFF) as g:
                for u in range(3):
                    lo(g * (2 * UPC) + W_FFN, u)
                glu_up(g - 1)
                lo(g * (2 * UPC) + W_FFN, 3)
                glu_low(g - 1)
                for u in range(4, UPC + 3):
                    lo(g * (2 * UPC) + W_FFN, u)
                glu_gate(g)
                for u in range(UPC + 3, 2 * UPC):
                    lo(g * (2 * UPC) + W_FFN, u)
            for u in range(3):
                lo(W_DOWN, u)
            glu_up(NFF - 1)
            lo(W_DOWN, 3)
            glu_low(NFF - 1)
            with dve.Fori(1, 2 * FC // 4) as j:
                for u in range(4):
                    lo(j * 4 + W_DOWN, u)

            for q in add_norm(F_HI, vec2[:, V2["post_ffn"]:V2["post_ffn"] + KC], 5 * KC, F_LO, 4,
                              4 * (NIN + NOUT) + KC, 8, 4):
                pass
            n = 0
            for t0, nt, dst in y_jobs:
                for q in range(4):
                    if q % 2:
                        dve.wait_ge(y_tr, n + 1)
                        v.tensor_copy(dst(q), ps[0:nt, 2 + n % 4, :]).then_inc(y_dve, 1)
                    n += 1

        @block.tensor
        def _(pe):
            mm = nc.tensor.matmul
            tr = nc.tensor.transpose
            pe.wait_ge(consts, 1)
            pe.wait_ge(silu_c, 2)
            for k in range(KC):
                ins = tr(ps[:, 7, k * NC:(k + 1) * NC], CR[:, k * P:(k + 1) * P], ident[0:NC, 0:NC])
            ins.then_inc(tr_done, 1)
            pe.wait_ge(vec_in, 16 * 8)
            tr(ps[:, 5, 0:NMOD + KC], VR[0:NMOD + KC, 0, :], ident[0:NMOD + KC, 0:NMOD + KC])
            tr(ps[:, 5, 128:128 + NV2], VR[0:NV2, 1, :], ident[0:NV2, 0:NV2]).then_inc(tr_done, 1)
            pe.wait_ge(x_in, 16 * (TB + 1))
            for k in range(KC):
                if k >= 4:
                    pe.wait_ge(x_dve if k % 2 else x_act, (k - 4) // 2 + 1)
                for tb in range(TB):
                    tr(ps[:, k % 4, tb * P:(tb + 1) * P], XR[:, tb, k * P:(k + 1) * P], ident[:, :])
                tr(ps[:, k % 4, TP:T], XS[:, k * P:(k + 1) * P], ident[0:TS, 0:TS]).then_inc(tr_done, 1)

            def sums(src, bank, n0, done):
                for q in range(4):
                    pe.wait_ge(sq_ready, n0 + q + 1)
                    for k in range(4 * q, 4 * q + 4):
                        ins = mm(ps[:, bank, 0:T], ones[:, :], src[:, k, :], start=(k == 0), stop=(k == KC - 1))
                ins.then_inc(done, 1)

            sums(F_LO, 6, 0, sums_done)

            def ada_block(ring, slot, a):
                for j in range(4):
                    ins = mm(ps[32 * j:32 * j + 32, 4, :], CTK[:, 4 * a + j, :],
                             ring[:, slot, j * CG:(j + 1) * CG], start=(a == 0), stop=(a == 3))
                return ins

            def mod_turn(done):
                for m in range(4):
                    ins = mm(ps[:, 5, m * NC:(m + 1) * NC], MROW[:, m * P:(m + 1) * P], sel_c[:, :],
                             start=True, stop=True)
                ins.then_inc(done, 1)

            def ada_group(g):
                for a in range(4):
                    pe.wait_ge(ad4_in[a], g * 16 + 16)
                    ada_block(AD4, a, a).then_inc(ad4_used, 1)
                pe.wait_ge(modrow_a, g + 1)

            pe.wait_ge(ct_ready, 1)
            pe.wait_ge(vec_ready, 2)
            ada_group(0)
            mod_turn(modt_a)
            with pe.Fori(1, NMA) as g:
                ada_group(g)
                pe.wait_ge(mod_a, g)
                mod_turn(modt_a)

            def split_products(out, k, w_hi, w_lo, xh, xl, first, last):
                mm(out, w_hi, xh[:, k, :], start=first, stop=False)
                mm(out, w_hi, xl[:, k, :], start=False, stop=False)
                return mm(out, w_lo, xh[:, k, :], start=False, stop=last)

            def unit(u, nb, bank0, first, last, free=None, k0=None, done=None):
                pe.wait_ge(lo_ready, nb + (u + 1))
                s = u % 4
                for m in range(MT):
                    if first and free is not None:
                        free(m)
                    for kk in range(2):
                        cs = slice(kk * CG + m * P, kk * CG + (m + 1) * P)
                        ins = split_products(ps[:, bank0 + m, 0:T], 2 * u + kk if k0 is None else k0 + kk,
                                             HI[:, s, cs], LO[:, s, cs], H_HI, H_LO,
                                             first and kk == 0, last and kk == 1)
                    if last and done is not None and m < MT - 1:
                        ins.then_inc(done, 1)
                ins.then_inc(unit_used, 1)

            def group(g, w0, cg, row0, h0=None, free=None):
                for u in range(UPC):
                    if h0 is not None and u % 2 == 0:
                        pe.wait_ge(h_ready, h0 + u // 2 + 1)
                    unit(u, g * UPC + w0, 0, u == 0, u == UPC - 1, free, done=bank_done)
                    if u == 3 and row0 is not None:
                        mod_turn(modt_b)
                    if u % 2:
                        a = u // 2
                        pe.wait_ge(ada_in[a % 2], cg * 32 + (16 * (a // 2) + 16))
                        if a == 0 and row0 is not None:
                            pe.wait_ge(modrow_b, row0)
                        ada_block(ADA, a % 2, a).then_inc(ada_used, 1)

            pe.wait_ge(mod_a, NMA)
            group(0, 0, 0, None, 0, None)
            with pe.Fori(1, NIN) as g:
                group(g, 0, g, g, None, lambda m: pe.wait_ge(bank_out, g * MT + (m - MT + 1)))
            pe.wait_ge(modrow_b, NIN)
            mod_turn(modt_b)
            pe.wait_ge(wg_split, 2)
            for k in range(KC):
                ins = split_products(ps[0:RANK, 6, 0:T], k, WGH[:, k, :], WGL[:, k, :], H_HI, H_LO,
                                     k == 0, k == KC - 1)
            ins.then_inc(glow_mm, 1)

            def tok(j, job):
                chunks, t0, nt, dst = job
                for i, c in enumerate(chunks):
                    ins = tr(ps[0:nt, j % 4, i * P:(i + 1) * P], PROJ[:, c, t0:t0 + nt], ident[:, :])
                ins.then_inc(tok_tr, 1)

            pe.wait_ge(bank_out, NIN * MT)
            for j, job in enumerate(tok_jobs):
                if j >= 4:
                    pe.wait_ge(tok_dve if j % 2 else tok_act, (j - 4) // 2 + 1)
                tok(j, job)
            pe.wait_ge(tok_act, NTOK // 2)
            pe.wait_ge(tok_dve, NTOK // 2)
            pe.wait_ge(mod_b, NIN)
            pe.wait_ge(consts, 3)

            def q_bcast(b):
                if b >= 1:
                    pe.wait_ge(qb_ready, b)
                mm(ps[:, 4, :], SELB[:, b, :], QTOK[:, 0:512], start=True, stop=True)
                mm(ps[:, 5, :], SELB[:, b, :], QTOK[:, 512:1024], start=True, stop=True).then_inc(qb_mm, 1)

            q_bcast(0)
            for h in range(H):
                if h >= 1:
                    pe.wait_ge(sb_abs, h)
                mm(ps[:, 0, 0:TP], PROJ[:, C_K + h, 0:P], PROJ[:, C_Q + h, 0:TP], start=True, stop=True)
                mm(ps[:, 0, TP:384], PROJ[:, C_K + h, P:TP], PROJ[:, C_Q + h, P:TP], start=True, stop=True)\
                    .then_inc(sb_z, 1)
                if h + 1 < TS:
                    q_bcast(h + 1)
                pe.wait_ge(sb_sp, h + 1)
                mm(ps[:, 1, 0:384], triu[:, :], SP[:, :], start=True, stop=False)
                mm(ps[:, 1, P:TP], ones[:, :], SP[:, TP:384], start=False, stop=True).then_inc(sb_tail, 1)
                pe.wait_ge(sb_a, h + 1)
                if h >= 1:
                    pe.wait_ge(sb_out, h)
                mm(ps[:, 2, 0:TP], VTOK[:, 0, h * DH:(h + 1) * DH], SA[:, 0:TP], start=True, stop=False)
                mm(ps[:, 2, P:TP], VTOK[:, 1, h * DH:(h + 1) * DH], SA[:, TP:384], start=False, stop=True)\
                    .then_inc(sb_o, 1)

            pe.wait_ge(sb_out, H)
            tok(NTOK, tok2_jobs[0])
            tok(NTOK + 1, tok2_jobs[1])
            pe.wait_ge(d_sp, 1)
            tok(NTOK + 2, tok2_jobs[2])
            mm(ps[:, 1, :], triu[:, :], ZD[:, :, :].rearrange("p b n -> p (b n)"), start=True, stop=False)
            mm(ps[:, 1, :], ones[:, :], DR[:, :, :, :].rearrange("p b g h -> p (b g h)"), start=False, stop=True)\
                .then_inc(d_tail, 1)
            pe.wait_ge(tok_act, NTOK // 2 + 2)
            pe.wait_ge(tok_dve, NTOK // 2 + 1)
            pe.wait_ge(d_arg, 1)
            pe.wait_ge(glow_ready, 1)
            pe.wait_ge(misc_in, 64)
            for h in range(GH):
                mm(ps[:, h, 0:T], WGU[:, h * DK:(h + 1) * DK], GLOW[:, :], start=True, stop=True).then_inc(g_mm, 1)

            def values(b):
                if b >= 1:
                    pe.wait_ge(v_evac, b)
                for grp in range(2):
                    for j in range(4):
                        pg = 4 * grp + j
                        pe.wait_ge(page_in[pg], 16 * (TS + b + 1))
                        for half in range(2):
                            ins = mm(ps[32 * j:32 * j + 32, 4 + half, :], AD[:, b, 32 * grp:32 * grp + 32],
                                     PG[:, pg, half * 512:half * 512 + 512], start=(grp == 0), stop=(grp == 1))
                        if pg < PAGES - 1:
                            ins.then_inc(page_used, 1)
                ins.then_inc(v_done, 1)

            def select(b):
                pe.wait_ge(v_evac, b + 1)
                if b >= 1:
                    pe.wait_ge(v_put, b)
                for h in range(H):
                    ins = mm(ps[:, 6, h:h + 1], DOUT[:, h * DH:(h + 1) * DH], sel_h[:, h:h + 1], start=True, stop=True)
                ins.then_inc(v_sel, 1)

            def tick(i):
                if i in V_TICK:
                    b = V_TICK[i]
                    if b >= 1:
                        select(b - 1)
                    values(b)

            pe.wait_ge(d_a, 1)
            pe.wait_ge(consts, 4)
            pe.wait_ge(g_qt, 1 + GH)
            for i in range(1, NSUB):
                pe.wait_ge(g_kd, i)
                kv = kview(i)
                lim = SUB * i
                for h in range(GH):
                    q = QT[:, h, lim:lim + SUB]
                    m0 = min(P, lim)
                    ins = mm(ps[0:m0, h, lim:lim + SUB], kv[:, h, 0:m0], q, start=True, stop=True)
                    if lim > P:
                        ins = mm(ps[0:lim - P, h, P + lim:P + lim + SUB], kv[:, h, P:lim], q, start=True, stop=True)
                ins.then_inc(g_off, 1)
                tick(i)
            pe.wait_ge(g_kd, NSUB)
            pe.wait_ge(g_offev, GH)
            kf = kview(NSUB)
            for j in range(2):
                for i in range(4):
                    h, tb = (4 * j + i) // 2, i % 2
                    ins = tr(ps[:, 2 + j, i * P:(i + 1) * P], kf[:, h, tb * P:(tb + 1) * P], ident[:, :])
                ins.then_inc(g_kft, 1)
            tick(NSUB)
            for t in range(SUB):
                if t == 2 or t == 3:
                    pe.wait_ge(g_kftev, 2)
                    for e in range(2):
                        h = 2 * (t - 2) + e
                        for tb in range(TB):
                            i = 2 * h + tb
                            ins = mm(ps[:, t, e * DV:(e + 1) * DV], KFT[:, i * P:(i + 1) * P],
                                     VG[:, tb, h * DV:(h + 1) * DV], start=(tb == 0), stop=(tb == TB - 1))
                    ins.then_inc(g_st, 1)
                pe.wait_ge(g_dprod, t + 1)
                w = SUB - t
                for e in range(2):
                    n = 2 * NSUB
                    ins = mm(ps[:, e, :].rearrange("p (b n) -> p b n", n=SUB)[:, :, t:SUB],
                             ZSEL[:, SUB - 1 - t:SUB - 1 - t + P],
                             dview(t)[:, e * n:(e + 1) * n, :], start=(t == 0), stop=(t == SUB - 1))
                ins.then_inc(g_diag, 1)
                tick(NSUB + 1 + t)
            pe.wait_ge(g_stev, 2)
            for h in range(GH):
                pe.wait_ge(g_att, h + 1)
                if h >= 2:
                    pe.wait_ge(g_oev, h - 1)
                at = ATT[:, h, :, :].rearrange("p a b -> p (a b)")
                for vb in range(VD):
                    o = vb * TP
                    cs = slice(h * DV + vb * P, h * DV + (vb + 1) * P)
                    mm(ps[:, 2 + h % 2, o:o + TP], VG[:, 0, cs], at[:, 0:TP], start=True, stop=False)
                    ins = mm(ps[:, 2 + h % 2, o + P:o + TP], VG[:, 1, cs], at[:, TP:384], start=False, stop=True)
                ins.then_inc(g_o, 1)
            pe.wait_ge(g_oev, GH)
            for h in range(GH):
                pe.wait_ge(km_ready, h + 1)
                for b in range(TS):
                    if h >= 1 and b % 2 == 0:
                        pe.wait_ge(snew, (h - 1) * TS + b + 2)
                    ins = mm(ps[:, b // 2, (b % 2) * DV:(b % 2) * DV + DV], KM[:, b, :], VGS[:, h * DV:(h + 1) * DV],
                             start=True, stop=True)
                    if b % 2:
                        ins.then_inc(skv, 1)
                pe.wait_ge(snew, (h + 1) * TS)
                if h >= 1:
                    pe.wait_ge(s_oev, h)
                for vb in range(VD):
                    for b in range(TS):
                        ins = mm(ps[:, 7, vb * TS + b:vb * TS + b + 1], SS[:, h % 2, b, vb * P:(vb + 1) * P],
                                 QS[:, h, b:b + 1], start=True, stop=True)
                ins.then_inc(s_o, 1)
            select(TS - 1)

            for q in range(4):
                pe.wait_ge(msq, q + 1)
                if q >= 2:
                    pe.wait_ge(h32_ready, 4 + q - 1)
                b0 = 4 * (q % 2)
                for c in range(4):
                    bank = b0 + (c if q < 2 else c // 2)
                    f = q < 2 or c % 2 == 0
                    e = q < 2 or c % 2 == 1
                    if q == 1 and c == 0:
                        pe.wait_ge(v_put, TS)
                    ins = mm(ps[:, bank, 0:T], ones[:, :], F_LO[:, 4 * q + c, :], start=f, stop=e)
                ins.then_inc(msum, 1)

            pe.wait_ge(h_ready, 8)
            group(0, W_OUT, NIN, None, 4, None)
            with pe.Fori(1, NOUT) as g:
                group(g, W_OUT, g + NIN, g + NIN, None, lambda m: pe.wait_ge(bank_out, g * MT + (NIN * MT + m - MT + 1)))
            pe.wait_ge(modrow_b, NIN + NOUT)
            mod_turn(modt_b)
            sums(SQD, 6, 4, sums_done)
            sums(SQD, 7, 8, sums_done)

            def ffn_group(g, first):
                nb = g * (2 * UPC) + W_FFN
                for u in range(UPC):
                    if first and u % 2 == 0:
                        pe.wait_ge(h_ready, 8 + u // 2 + 1)
                    unit(u, nb, 0, u == 0, u == UPC - 1,
                         None if first else lambda m: pe.wait_ge(glu_step, g * 4 - 1))
                for u in range(UPC):
                    unit(u + UPC, nb, MT, u == 0, u == UPC - 1,
                         None if first else lambda m: pe.wait_ge(glu_step, g * 4), k0=2 * u)

            ffn_group(0, True)
            with pe.Fori(1, NFF) as g:
                ffn_group(g, False)

            def down(k, nb, half, first, last, u):
                pe.wait_ge(lo_ready, nb + (u + 1))
                if half == 0 and u == 0:
                    pe.wait_ge(glu_done, (nb - W_DOWN) // 4 + 1 if isinstance(nb, int) else DONE[0])
                for m in range(8):
                    if first:
                        if half == 0:
                            pe.wait_ge(glu_step, NFF * 4 - 1 if m < 4 else NFF * 4)
                        else:
                            pe.wait_ge(bank_out, (NIN + NOUT) * MT + m + 1)
                    cs = slice(m * P, (m + 1) * P)
                    xh = A_HI[:, bass.ds(k, 1), :].rearrange("p o t -> p (o t)")
                    xl = A_LO[:, bass.ds(k, 1), :].rearrange("p o t -> p (o t)")
                    out = ps[:, m, 0:T]
                    mm(out, HI[:, u, cs], xh, start=first, stop=False)
                    mm(out, HI[:, u, cs], xl, start=False, stop=False)
                    ins = mm(out, LO[:, u, cs], xh, start=False, stop=last)
                    if last and m < 7:
                        ins.then_inc(bank_done, 1)
                ins.then_inc(unit_used, 1)

            DONE = [None]
            for half in range(2):
                w0 = W_DOWN + half * FC
                for u in range(4):
                    down(u, w0, half, u == 0, False, u)
                with pe.Fori(1, FC // 4 - 1) as j:
                    DONE[0] = j + 1
                    for u in range(4):
                        down(j * 4 + u, j * 4 + w0, half, False, False, u)
                for u in range(4):
                    down(FC - 4 + u, w0 + FC - 4, half, False, u == 3, u)

            sums(F_LO, 6, 12, sums_done)
            pe.wait_ge(x_new, 8)
            n = 0
            for t0, nt, dst in y_jobs:
                for q in range(4):
                    if n >= 4:
                        pe.wait_ge(y_dve if q % 2 else y_act, (n - 4) // 2 + 1)
                    for i in range(4):
                        ins = tr(ps[0:nt, 2 + n % 4, i * P:(i + 1) * P], X[:, 4 * q + i, t0:t0 + nt], ident[:, :])
                    ins.then_inc(y_tr, 1)
                    n += 1


_INS = ["x_prompt", "x_sample", "c_prompt", "c_sample", "cache_k", "cache_v", "page_table", "state_gla", "w_ada",
        "b_ada", "g_pre_mix", "w_in", "b_sb", "w_gate_up", "b_gate", "g_sb_out", "g_gla_out", "w_out", "g_post_mix",
        "g_pre_ffn", "w_ffn_gate", "w_ffn_up", "w_ffn_down", "g_post_ffn"]


def kernel(**inputs):
    import numpy as np
    import concourse.bacc as bacc
    from concourse.bass_utils import run_bass_kernel_spmd as run

    nc = bacc.Bacc("TRN2", target_bir_lowering=False, num_devices=1)
    arrays, args = {}, []
    for name in _INS:
        a = np.ascontiguousarray(inputs[name])
        arrays[f"in_{name}"] = a
        args.append(nc.dram_tensor(f"in_{name}", a.shape, mybir.dt.from_np(a.dtype), kind="ExternalInput").ap())
    batch, seq, width = inputs["x_prompt"].shape
    rows = inputs["x_sample"].shape[0]
    depth, _, _, heads, head_dim = inputs["cache_k"].shape
    gla = inputs["state_gla"].shape[2:]
    outs = [(batch, seq, width), (rows, 1, width),
            (depth, batch, seq, heads, head_dim), (depth, batch, seq, heads, head_dim), (depth, batch, *gla),
            (depth, rows, 1, heads, head_dim), (depth, rows, 1, heads, head_dim), (depth, rows, *gla)]
    for i, shape in enumerate(outs):
        args.append(nc.dram_tensor(f"out_{i}", shape, F32, kind="ExternalOutput").ap())
    stickbreak_gla_layer(nc, *args)
    r = run(nc, [arrays], core_ids=[0])
    return tuple(r.results[0][f"out_{i}"] for i in range(len(outs)))
```

```python
from contextlib import ExitStack

import concourse.bass as bass
from concourse import mybir

F32 = mybir.dt.float32
F32R = mybir.dt.float32r
I32 = mybir.dt.int32
ACT = mybir.ActivationFunctionType
ALU = mybir.AluOpType
AX = mybir.AxisListType

P = 128
EPS = 1e-6
BIG = 30000.0


def stickbreak_gla_layer(nc, x_prompt, x_sample, c_prompt, c_sample, cache_k, cache_v, page_table, state_gla,
                         w_ada, b_ada, g_pre_mix, w_in, b_sb, w_gate_up, b_gate, g_sb_out, g_gla_out, w_out,
                         g_post_mix, g_pre_ffn, w_ffn_gate, w_ffn_up, w_ffn_down, g_post_ffn,
                         y_prompt, y_sample, new_k_prompt, new_v_prompt, new_state_prompt,
                         new_k_sample, new_v_sample, new_state_sample):
    D = x_prompt.shape[2]
    TP = x_prompt.shape[1]
    TS = x_sample.shape[0]
    T = TP + TS
    TB = TP // P
    KC = D // P
    H = b_sb.shape[1]
    DH = g_sb_out.shape[1]
    GH, DK, DV = state_gla.shape[2:]
    RANK = w_gate_up.shape[1]
    NPOOL = cache_k.shape[1]
    PAGES = page_table.shape[1]
    FF = w_ffn_gate.shape[2]
    FC = FF // P
    NMOD = w_ada.shape[2] // P
    NC = 1 + TS
    CG = 512
    MT = CG // P
    NIN = (w_in.shape[2] - RANK) // CG
    NOUT = D // CG
    NFF = FF // CG
    UPC = KC // 2
    NMA = 2 * D // CG
    NMC = 4
    NMB = 6 * D // CG - NMA - NMC - NOUT
    HS = H * DH
    C_Q, C_K, C_V = 0, H, 2 * H
    C_GQ, C_GK, C_GV = 3 * H, 3 * H + GH, 3 * H + 2 * GH
    C_GR = C_GV + GH * DV // P
    NPROJ = C_GR + GH * DV // P
    SB_SCALE = float(DH) ** -0.5
    GLA_SCALE = float(DK) ** -0.5
    SUB = 16
    NSUB = TP // SUB
    VD = DV // P
    assert (D, TP, TS, H, DH, GH, DK, DV, PAGES, KC) == (2048, 256, 8, 8, 128, 4, 128, 256, 8, 16)

    ctx = ExitStack()
    with ctx:
        def sem(name):
            return ctx.enter_context(nc.semaphore(name))

        base = -(-nc.sbuf_base // 64) * 64
        slab_words = (nc.sbuf_usable_end - base) // 4 // 16 * 16
        ctx.enter_context(nc.sbuf_tensor("slab", [P, slab_words], F32))
        top = base + slab_words * 4
        cursor = [base]

        def put(name, shape, dt=F32, at=None):
            size = 4
            for s in shape[1:]:
                size *= s
            size = -(-size // 32) * 32
            if at is None:
                at = cursor[0]
                cursor[0] += size
            assert at + size <= top, (name, at + size, top)
            return nc.alloc_sbuf_tensor_at(name, shape, dt, offset=at), at + size

        RAW, _ = put("raw", [P, 4, 1024])
        at_split = cursor[0]
        HI, _ = put("w_hi", [P, 4, 1024], F32R)
        LO, _ = put("w_lo", [P, 4, 1024], F32R)
        at_h = cursor[0]
        H_HI, _ = put("h_hi", [P, KC, T], F32R)
        at_hlo = cursor[0]
        H_LO, _ = put("h_lo", [P, KC, T], F32R)
        X, _ = put("x_t", [P, KC, T])
        MOD, _ = put("mod_t", [P, NMOD, NC])
        ident, _ = put("ident", [P, P])
        ones, _ = put("ones", [P, P])
        triu, _ = put("triu", [P, P])
        vec1, _ = put("vec1", [P, NMOD + KC])
        vec2, _ = put("vec2", [P, 56])
        scale_t, _ = put("scale_t", [P, KC, NC])
        at_rstd = cursor[0]
        rstd, _ = put("rstd", [P, T])
        assert cursor[0] == at_rstd + T * 4
        rvar, _ = put("rvar", [P, T])
        sel_c, _ = put("sel_c", [P, NC])
        sel_h, _ = put("sel_h", [P, H])
        bias_h, _ = put("bias_h", [P, H])
        NRM = H + GH
        mean_sel, _ = put("mean_sel", [P, 2, 2 * NRM - 1])
        r0 = cursor[0]

        A_HI, e1 = put("act_hi", [P, FC, T], F32R, at=r0)
        A_LO, e1 = put("act_lo", [P, FC, T], F32R, at=e1)
        GLU, e1 = put("glu", [P, MT, T], at=e1)
        F_HI, _ = put("f_hi", [P, KC, T], at=at_h)
        F_LO, _ = put("f_lo", [P, KC, T], at=at_hlo)
        PG, _ = put("pages", [P, 8, 1024], at=at_h)
        ADC, _ = put("ada_c", [P, 4, 2048], at=at_h)
        PROJ, rc = put("proj_t", [P, NPROJ, T], at=r0)
        MIX = PROJ[:, 0:KC, :]
        MT_ = PROJ[:, KC:2 * KC, :]
        SQD = PROJ[:, 2 * KC:3 * KC, :]
        AD4, a1 = put("ada4", [P, 4, 2048], at=r0)
        XR, a1 = put("x_rows", [P, 2, D], at=a1)
        ADA, b1 = put("ada2", [P, 2, 2048], at=rc)
        MROW, b1 = put("mod_row", [P, CG], at=b1)
        KP, b2 = put("k_pages", [P, 4, 1024], at=b1)
        XS, b1 = put("xs_rows", [TS, D], at=b1)
        CR, b1 = put("c_rows", [NC, D], at=b1)
        assert b1 == b2
        CE, vr = put("c_exp", [P, KC * NC], at=rc)
        VR, _ = put("vec_rows", [P, 2, P], at=vr)
        WG, b1 = put("w_glow", [P, KC, RANK], at=b1)
        WGH, b1 = put("w_glow_hi", [P, KC, RANK], F32R, at=b1)
        WGL, b1 = put("w_glow_lo", [P, KC, RANK], F32R, at=b1)
        QBC, b1 = put("q_bcast", [P, 2, HS], at=b1)
        ZD, b1 = put("z_dec", [P, TS, PAGES * H], at=b1)
        at_rvar = at_rstd + T * 4
        ZS, z1 = put("z_stage", [P, PAGES * H], at=at_rvar)
        QB, z1 = put("q_cols", [P, 2, H], at=z1)
        GLOW, c0 = put("g_low", [RANK, T], at=top - 1088)
        WGU, c0 = put("w_gate_up_s", [RANK, GH * DK], at=top - 1088 - 2048)
        PT, c0 = put("page_t", [1, TS * PAGES], I32, at=top - 1088 - 2048 - 256)
        c_top = top - 1088 - 2048 - 256
        CTK, _ = put("c_t_keep", [P, KC, 32], at=c_top - 2048)
        c_top -= 2048
        assert b1 <= c_top, (b1, c_top)

        VTOK, c1 = put("v_tok", [P, TB, HS], at=rc)
        VG, c1 = put("vg_tok", [P, TB, GH * DV], at=c1)
        ZB, c1q = put("sb_z", [P, 2, 2, 384], at=c1 + TS * PAGES * H * 4)
        SE, c1q = put("sb_e", [P, 2, 2, 384], at=c1q)
        SA, c1q = put("sb_a", [P, 2, 2, 384], at=c1q)
        SP, c1q = put("sb_sp", [P, 2, 2, 384], at=c1q)
        M01, c1q = put("mask01", [P, 384], at=c1q)
        MNEG, c1q = put("maskneg", [P, 384], at=c1q)
        assert c1q <= b1 - TS * PAGES * H * 4, (c1q, b1)
        KTOK, s1 = put("k_tok", [P, TB, HS], at=at_split)
        KST, s1 = put("ks_tok", [TS, HS], at=s1)
        VST, s1 = put("vs_tok", [TS, HS], at=s1)
        AD, g1 = put("a_dec", [P, TS, PAGES * H], at=c1)
        CB0, g1 = put("cum0", [P, GH, TP], at=g1)
        CB1, g1 = put("cum1", [P, GH, TP], at=g1)
        CAB, g1 = put("cum_abs", [P, GH, TP], at=g1)
        QT, g1 = put("gla_q", [P, GH, TP], at=g1)
        KD, g1 = put("gla_kd", [P, 2, GH * TP], at=g1)
        BX, g1 = put("cum_blk", [P, GH, NSUB + 1], at=g1)
        GATE, g1 = put("gate", [P, GH, T], at=g1)
        at_kd = c1 + 2048 + 4 * 4096
        GT, _ = put("gate_t", [P, GH, T], at=at_kd)
        DIAG_T, _ = put("diag_t", [P, TP], at=at_kd + 4096)
        MIXR, _ = put("mix_rstd", [P, 4, T], at=at_kd)
        assert g1 <= c_top, (g1, c_top)
        off_v = r0 + C_V * T * 4
        DR, _ = put("dec_r", [P, TS, PAGES, H], at=off_v)
        DOUT, dv1 = put("dec_out", [P, HS], at=off_v)
        BD, dv1 = put("blockdiag", [P, P], at=dv1)
        ZSEL, dv1 = put("zsel", [P, P + SUB], at=dv1)
        QS, dv1 = put("qs_scaled", [P, GH, TS], at=dv1)
        ALP, dv1 = put("alpha", [P, GH, TS], at=dv1)
        RT, dv1 = put("gate_exp", [P, 2, T], at=dv1)
        DO, dv1 = put("dec_gla_out", [P, GH, VD * TS], at=dv1)
        DIAG, _ = put("diag", [P, 2, GH * TP], at=r0 + C_K * T * 4)
        GE, _ = put("gate_e", [P, GH, T], at=r0 + C_K * T * 4)
        GL, _ = put("gate_l", [P, GH, T], at=r0 + (C_K + GH) * T * 4)
        assert dv1 <= off_v + 8 * T * 4
        SS, q1 = put("state_s", [P, 2, TS, DV], at=at_split)
        ATT, q1 = put("att", [P, GH, 3, P], at=q1)
        KGS, q1 = put("kgs_tok", [TS, GH * DK], at=q1)
        VGS, q1 = put("vgs_tok", [TS, GH * DV], at=q1)
        KM, q1 = put("kgs_masked", [TS, TS, DK], at=q1)
        assert q1 <= at_h, (q1, at_h)
        SFIN = KD[:, 0, :].rearrange("p (h v) -> p h v", h=GH)
        KFT = KD[:, 1, :]
        SIL = PROJ[:, C_GR:C_GR + GH * VD, :]
        YROW, yy = put("y_rows", [P, TB, D], at=r0)
        YS, yy = put("y_s_rows", [TS, D], at=yy)
        y_jobs = [(tb * P, P, lambda q, tb=tb: YROW[:, tb, q * 512:q * 512 + 512]) for tb in range(TB)]
        y_jobs.append((TP, TS, lambda q: YS[:, q * 512:q * 512 + 512]))

        ps = ctx.enter_context(nc.psum_tensor("ps", [P, 8, 512], F32))

        win_v = w_in[0].rearrange("(k p) n -> p k n", p=P)
        wout_v = w_out[0].rearrange("(k p) n -> p k n", p=P)
        wg_v = w_ffn_gate[0].rearrange("(k p) n -> p k n", p=P)
        wu_v = w_ffn_up[0].rearrange("(k p) n -> p k n", p=P)
        wd_v = w_ffn_down[0].rearrange("(k p) n -> p k n", p=P)
        ada_v = w_ada[0].rearrange("(k p) n -> p k n", p=P)
        pool_k = cache_k[0].rearrange("n p h d -> n p (h d)")
        pool_v = cache_v[0].rearrange("n p h d -> n p (h d)")

        c_in = sem("c_in")
        x_in = sem("x_in")
        vec_in = sem("vec_in")
        misc_in = sem("misc_in")
        raw_in = [sem(f"raw_in{s}") for s in range(4)]
        ad4_in = [sem(f"ad4_in{s}") for s in range(4)]
        adc_in = [sem(f"adc_in{s}") for s in range(4)]
        ada_in = [sem(f"ada_in{s}") for s in range(2)]
        kpage_in = [sem(f"kpage_in{s}") for s in range(4)]
        vpage_in = [sem(f"vpage_in{s}") for s in range(8)]
        state_in = [sem(f"state_in{s}") for s in range(2)]
        state_out = [sem(f"state_out{s}") for s in range(2)]
        consts = sem("consts")
        hi_ready = sem("hi_ready")
        lo_ready = sem("lo_ready")
        unit_used = sem("unit_used")
        bank_done = sem("bank_done")
        bank_out = sem("bank_out")
        ad4_used = sem("ad4_used")
        ada_used = sem("ada_used")
        adc_used = sem("adc_used")
        modrow_c = sem("modrow_c")
        modt_c = sem("modt_c")
        mod_c = sem("mod_c")
        modrow_a = sem("modrow_a")
        modrow_b = sem("modrow_b")
        modt_a = sem("modt_a")
        modt_b = sem("modt_b")
        mod_a = sem("mod_a")
        mod_b = sem("mod_b")
        act_own = sem("act_own")
        dve_own = sem("dve_own")
        pool_own = sem("pool_own")
        silu_c = sem("silu_c")
        tr_done = sem("tr_done")
        ct_ready = sem("ct_ready")
        x_act = sem("x_act")
        x_dve = sem("x_dve")
        vec_ready = sem("vec_ready")
        sq_ready = sem("sq_ready")
        sums_done = sem("sums_done")
        h_ready = sem("h_ready")
        h32_ready = sem("h32_ready")
        hhi_ready = sem("hhi_ready")
        glow_mm = sem("glow_mm")
        wg_split = sem("wg_split")
        glow_ready = sem("glow_ready")
        tok_tr = sem("tok_tr")
        tok_act = sem("tok_act")
        tok_dve = sem("tok_dve")
        kv_out = sem("kv_out")
        kv_outb = sem("kv_outb")
        qb_mm = sem("qb_mm")
        qb_ready = sem("qb_ready")
        kpage_used = sem("kpage_used")
        vpage_used = sem("vpage_used")
        q_col = sem("q_col")
        sb_z = sem("sb_z")
        sb_abs = sem("sb_abs")
        sb_ln = sem("sb_ln")
        sb_sp = sem("sb_sp")
        sb_tail = sem("sb_tail")
        sb_arg = sem("sb_arg")
        sb_a = sem("sb_a")
        sb_o = sem("sb_o")
        sb_out = sem("sb_out")
        zs_taken = sem("zs_taken")
        d_a = sem("d_a")
        v_evac = sem("v_evac")
        v_sel = sem("v_sel")
        v_put = sem("v_put")
        g_mm = sem("g_mm")
        g_abs = sem("g_abs")
        g_ln = sem("g_ln")
        g_cum = sem("g_cum")
        g_eq = sem("g_eq")
        g_qt = sem("g_qt")
        g_kdiff = sem("g_kdiff")
        g_kexp = sem("g_kexp")
        g_kd = sem("g_kd")
        g_off = sem("g_off")
        g_offev = sem("g_offev")
        g_ddiff = sem("g_ddiff")
        g_dexp = sem("g_dexp")
        g_dprod = sem("g_dprod")
        g_diag = sem("g_diag")
        g_att = sem("g_att")
        g_o = sem("g_o")
        g_oev = sem("g_oev")
        g_kft = sem("g_kft")
        g_kftev = sem("g_kftev")
        g_st = sem("g_st")
        g_stev = sem("g_stev")
        g_stout = sem("g_stout")
        km_ready = sem("km_ready")
        dec_mm = sem("dec_mm")
        dec_taken = sem("dec_taken")
        silu_r = sem("silu_r")
        rs12_ready = sem("rs12_ready")
        norm_bc = sem("norm_bc")
        norm_sb = sem("norm_sb")
        alp_ready = sem("alp_ready")
        var_ready = sem("var_ready")
        rs_ready = sem("rs_ready")
        msq = sem("msq")
        msum = sem("msum")
        r_exp = sem("r_exp")
        glu_e = sem("glu_e")
        glu_step = sem("glu_step")
        glu_hi = sem("glu_hi")
        glu_done = sem("glu_done")
        y_tr = sem("y_tr")
        y_rows = sem("y_rows")
        y_out = sem("y_out")
        x_new = sem("x_new")

        W_OUT = NIN * UPC
        W_FFN = W_OUT + NOUT * UPC
        W_DOWN = W_FFN + 2 * NFF * UPC

        V_GPRE = NMOD
        V2 = dict(post_mix=0, pre_ffn=KC, post_ffn=2 * KC, b_gate=3 * KC, sb=3 * KC + GH, gla=3 * KC + GH + 1)
        NV2 = V2["gla"] + VD

        def linker(eng, own):
            n = [0]

            def link(ins):
                n[0] += 1
                ins.then_inc(own, 1)
                eng.wait_ge(own, n[0])
            return link

        tok_jobs = []
        for tb in range(TB):
            for half in range(2):
                tok_jobs.append(([C_K + 4 * half + j for j in range(4)], tb * P, P,
                                 KTOK[:, tb, half * 512:half * 512 + 512]))
            for half in range(2):
                tok_jobs.append(([C_V + 4 * half + j for j in range(4)], tb * P, P,
                                 VTOK[:, tb, half * 512:half * 512 + 512]))
            for half in range(2):
                tok_jobs.append(([C_GV + 4 * half + j for j in range(4)], tb * P, P,
                                 VG[:, tb, half * 512:half * 512 + 512]))
        for first, dst in ((C_K, KST), (C_V, VST)):
            for half in range(2):
                tok_jobs.append(([first + 4 * half + j for j in range(4)], TP, TS, dst[:, half * 512:half * 512 + 512]))
        NGS = MT + 3
        tok_jobs.append(([C_GK + j for j in range(4)], TP, TS, KGS[:, 0:512]))
        for half in range(2):
            tok_jobs.append(([C_GV + 4 * half + j for j in range(4)], TP, TS, VGS[:, half * 512:half * 512 + 512]))
        NTOK = len(tok_jobs)
        NTOK_ACT, NTOK_DVE = (NTOK + 1) // 2, NTOK // 2

        SB_PAIRS = H // 2
        SB_ITEMS = SB_PAIRS + 1

        DOT0 = NIN - TS

        V_TICK = {4 * b: b for b in range(TS)}

        PAIRS = TS // 2
        NEV = PAIRS + 1
        DEC_TICK = {1 + 3 * n // 2: n for n in range(GH * NEV)}
        SILU_TICK = {4 + c: c for c in range(GH * VD)}

        DEEP = 4
        LAG = DEEP - 1
        CB0F = CB0[:, :, :].rearrange("p h t -> p (h t)")
        GATEF = GATE[:, :, :].rearrange("p h t -> p (h t)")

        def kview(i):
            place = (KD[:, 0, :], KD[:, 1, :], CB0F, GATEF)[i % DEEP]
            return place[:, 0:GH * SUB * i].rearrange("p (h n) -> p h n", h=GH)

        def dview(t):
            place = (DIAG[:, 0, :], DIAG[:, 1, :], QT[:, :, :].rearrange("p h t -> p (h t)"),
                     CAB[:, :, :].rearrange("p h t -> p (h t)"))[t % DEEP]
            return place[:, 0:GH * NSUB * (SUB - t)].rearrange("p (b n) -> p b n", n=SUB - t)

        def dec_view(t):
            return t[:, 0, :, :].rearrange("p e n -> p (e n)")[:, 0:TS * PAGES * H]

        block = ctx.enter_context(nc.Block())

        @block.sync
        def _(sp):
            sp.dma_start(CR[0:1, :], c_prompt).then_inc(c_in, 16)
            sp.dma_start(CR[1:NC, :], c_sample).then_inc(c_in, 16)
            for tb in range(TB):
                sp.dma_start(XR[:, tb, :], x_prompt[0, tb * P:(tb + 1) * P, :]).then_inc(x_in, 16)
            sp.dma_start(XS[:, :], x_sample.rearrange("b o d -> (b o) d")).then_inc(x_in, 16)

            def ada_unit(g, a):
                return ada_v[:, 4 * a:4 * a + 4, bass.ds(g * CG, CG)]

            def dst4(t):
                return t.rearrange("p (k n) -> p k n", k=4)

            for a in range(4):
                sp.dma_start(dst4(AD4[:, a, :]), ada_unit(0, a)).then_inc(ad4_in[a], 16)
                if a == 0:
                    sp.dma_start(VR[0:NMOD, 0, :], b_ada.rearrange("o (k p) -> (o k) p", p=P)).then_inc(vec_in, 16)
                    sp.dma_start(VR[NMOD:NMOD + KC, 0, :],
                                 g_pre_mix.rearrange("o (k p) -> (o k) p", p=P)).then_inc(vec_in, 16)
                    for nme, t, n in (("post_mix", g_post_mix, KC), ("pre_ffn", g_pre_ffn, KC),
                                      ("post_ffn", g_post_ffn, KC), ("b_gate", b_gate, GH), ("sb", g_sb_out, 1),
                                      ("gla", g_gla_out, VD)):
                        sp.dma_start(VR[V2[nme]:V2[nme] + n, 1, :],
                                     t.rearrange("o (k p) -> (o k) p", p=P)).then_inc(vec_in, 16)
            sp.dma_start(bias_h[:, :], b_sb[0].partition_broadcast(P)).then_inc(misc_in, 16)
            sp.dma_start(WGU[:, :], w_gate_up[0]).then_inc(misc_in, 16)
            sp.dma_start(PT[:, :], page_table.rearrange("b n -> (b n)").unsqueeze(0)).then_inc(misc_in, 16)
            sp.dma_start(WG[:, :, :], win_v[:, :, NIN * CG:NIN * CG + RANK]).then_inc(misc_in, 16)
            def w_dst(s):
                return RAW[:, s, :].rearrange("p (k n) -> p k n", k=2)

            def w_unit(view, g, u, n):
                s = u % 4
                if n is not None:
                    sp.wait_ge(lo_ready, n)
                sp.dma_start(w_dst(s), view[:, 2 * u:2 * u + 2, bass.ds(g * CG, CG)]).then_inc(raw_in[s], 16)

            with sp.Fori(1, NMA) as g:
                for a in range(4):
                    sp.wait_ge(ad4_used, g * 4 + (a - 3))
                    sp.dma_start(dst4(AD4[:, a, :]), ada_unit(g, a)).then_inc(ad4_in[a], 16)
            for u in range(4):
                w_unit(win_v, 0, u, None)
            sp.wait_ge(ct_ready, 1)
            sp.wait_ge(vec_ready, 2)
            for u in range(UPC):
                if u >= 4:
                    w_unit(win_v, 0, u, u - 3)
                if u % 2:
                    a = u // 2
                    if a >= 2:
                        sp.wait_ge(ada_used, a - 1)
                    sp.dma_start(dst4(ADA[:, a % 2, :]), ada_unit(NMA, a)).then_inc(ada_in[a % 2], 16)
            with sp.Fori(1, NMB) as g:
                for u in range(UPC):
                    w_unit(win_v, g, u, g * UPC + (u - 3))
                    if u % 2:
                        a = u // 2
                        sp.wait_ge(ada_used, g * 4 + (a - 1))
                        sp.dma_start(dst4(ADA[:, a % 2, :]), ada_unit(g + NMA, a)).then_inc(ada_in[a % 2], 16)
            with sp.Fori(NMB, NIN) as g:
                for u in range(UPC):
                    w_unit(win_v, g, u, g * UPC + (u - 3))
            sp.wait_ge(glow_mm, 1)
            for a in range(4):
                sp.dma_start(dst4(ADC[:, a, :]), ada_unit(NMA + NMB, a)).then_inc(adc_in[a], 16)
            with sp.Fori(1, NMC) as g:
                for a in range(4):
                    sp.wait_ge(adc_used, g * 4 + (a - 3))
                    sp.dma_start(dst4(ADC[:, a, :]), ada_unit(g + (NMA + NMB), a)).then_inc(adc_in[a], 16)

            def v_pages(b, first):
                for j in range(PAGES):
                    page = sp.value_load(PT[0:1, bass.ds(b * PAGES + j, 1)], min_val=0, max_val=NPOOL - 1)
                    if first:
                        sp.wait_ge(adc_used, NMC * 4 - 3 + j // 2)
                    else:
                        sp.wait_ge(vpage_used, b * PAGES + (j - PAGES + 1))
                    sp.dma_start(PG[:, j, :], pool_v[bass.ds(page, 1), :, :].rearrange("o p n -> p (o n)"))\
                        .then_inc(vpage_in[j], 16)

            sp.wait_ge(misc_in, 64)
            v_pages(0, True)
            with sp.Fori(1, TS) as b:
                v_pages(b, False)
            for u in range(4):
                w_unit(wout_v, 0, u, W_OUT + u - 3)
            sp.wait_ge(kv_outb, 16 * TB)
            sp.wait_ge(v_put, TS)
            sp.wait_ge(g_oev, GH)
            sp.wait_ge(dec_taken, GH * NEV)
            sp.wait_ge(g_stout, 16)
            for u in range(UPC):
                if u >= 4:
                    w_unit(wout_v, 0, u, W_OUT + u - 3)
                if u % 2:
                    a = u // 2
                    sp.wait_ge(ada_used, NMB * 4 + a - 1)
                    sp.dma_start(dst4(ADA[:, a % 2, :]), ada_unit(NMA + NIN, a)).then_inc(ada_in[a % 2], 16)
            with sp.Fori(1, NOUT) as g:
                for u in range(UPC):
                    w_unit(wout_v, g, u, g * UPC + (W_OUT + u - 3))
                    if u % 2:
                        a = u // 2
                        sp.wait_ge(ada_used, g * 4 + (NMB * 4 + a - 1))
                        sp.dma_start(dst4(ADA[:, a % 2, :]), ada_unit(g + (NMA + NIN), a)).then_inc(ada_in[a % 2], 16)
            with sp.Fori(0, NFF) as g:
                for u in range(UPC):
                    w_unit(wg_v, g, u, g * 2 * UPC + (W_FFN + u - 3))
                for u in range(UPC):
                    w_unit(wu_v, g, u, g * 2 * UPC + (W_FFN + UPC + u - 3))
            for half in range(2):
                with sp.Fori(0, FC // 4) as j:
                    for u in range(4):
                        sp.wait_ge(lo_ready, j * 4 + (W_DOWN + half * FC + u - 3))
                        sp.dma_start(RAW[:, u, :].unsqueeze(1), wd_v[:, bass.ds(j * 4 + u, 1), half * 1024:half * 1024 + 1024])\
                            .then_inc(raw_in[u], 16)

            for q in range(4):
                cs = slice(q * 512, q * 512 + 512)
                for i, (t0, nt, dst) in enumerate(y_jobs):
                    sp.wait_ge(y_rows, q * len(y_jobs) + i + 1)
                    rows = y_prompt[0, t0:t0 + nt, cs] if t0 < TP else \
                        y_sample.rearrange("b o d -> (b o) d")[:, cs]
                    sp.dma_start(rows, dst(q)).then_inc(y_out, 16)
            sp.wait_ge(y_out, 16 * 4 * len(y_jobs))

        @block.gpsimd
        def _(pool):
            link = linker(pool, pool_own)
            g = nc.gpsimd
            link(g.memset(ident[:, :], 0.0))
            link(g.affine_select(out=ident[:, :], in_=ident[:, :], compare_op=ALU.not_equal, fill=1.0, base=0,
                                 pattern=[[-1, P]], channel_multiplier=1))
            link(g.memset(ones[:, :], 1.0))
            link(g.memset(sel_c[:, :], 0.0))
            for j in range(4):
                ins = g.affine_select(out=sel_c[:, :], in_=sel_c[:, :], compare_op=ALU.not_equal, fill=1.0,
                                      base=-32 * j, pattern=[[-1, NC]], channel_multiplier=1)
                if j < 3:
                    link(ins)
                else:
                    ins.then_inc(consts, 1)
            link(g.memset(mean_sel[:, :, :], 0.0))
            link(g.memset(mean_sel[:, 0, NRM - 1:NRM], 1.0 / DH))
            link(g.memset(mean_sel[:, 1, NRM - 1:NRM], 1.0 / DV))
            link(g.affine_select(out=triu[:, :], in_=ones[:, :], compare_op=ALU.is_ge, fill=0.0, base=0,
                                 pattern=[[-1, P]], channel_multiplier=1))
            link(g.memset(sel_h[:, :], 0.0))
            for j in range(4):
                ins = g.affine_select(out=sel_h[:, :], in_=sel_h[:, :], compare_op=ALU.not_equal, fill=1.0,
                                      base=-40 * j, pattern=[[-1, H]], channel_multiplier=1)
                if j < 3:
                    link(ins)
                else:
                    ins.then_inc(consts, 1)
            pool.wait_ge(misc_in, 64)
            pool.wait_ge(ct_ready, 1)
            pool.wait_ge(x_act, KC // 2)
            pool.wait_ge(x_dve, KC // 2)

            def k_pages(b, first):
                for j in range(PAGES):
                    page = pool.value_load(PT[0:1, bass.ds(b * PAGES + j, 1)], min_val=0, max_val=NPOOL - 1)
                    if not first or j >= 4:
                        pool.wait_ge(kpage_used, b * PAGES + (j - 3))
                    pool.dma_start(KP[:, j % 4, :], pool_k[bass.ds(page, 1), :, :].rearrange("o p n -> p (o n)"))\
                        .then_inc(kpage_in[j % 4], 16)

            k_pages(0, True)
            with pool.Fori(1, TS) as b:
                k_pages(b, False)
            pool.wait_ge(kpage_used, TS * PAGES)
            pool.wait_ge(unit_used, W_OUT)
            pool.wait_ge(glow_mm, 1)
            pool.wait_ge(mod_b, NMB)
            link(g.memset(M01[:, :], 1.0))
            for c in (0, 256):
                ins = g.affine_select(out=M01[:, c:c + P], in_=M01[:, c:c + P], compare_op=ALU.is_gt, fill=0.0,
                                      base=0, pattern=[[1, P]], channel_multiplier=-1)
                link(ins)
            g.tensor_scalar(MNEG[:, :], M01[:, :], BIG, -BIG, ALU.mult, ALU.add).then_inc(consts, 1)
            pool.wait_ge(tok_act, NTOK_ACT)
            pool.wait_ge(tok_dve, NTOK_DVE)
            for tb in range(TB):
                rows = slice(tb * P, (tb + 1) * P)
                pool.dma_start(new_k_prompt[0, 0].rearrange("t h d -> t (h d)")[rows, :],
                               KTOK[:, tb, :]).then_inc(kv_out, 16)
                pool.dma_start(new_v_prompt[0, 0].rearrange("t h d -> t (h d)")[rows, :],
                               VTOK[:, tb, :]).then_inc(kv_outb, 16)
            pool.dma_start(new_k_sample[0].rearrange("b o h d -> (b o) (h d)"), KST[:, :]).then_inc(kv_out, 16)
            pool.dma_start(new_v_sample[0].rearrange("b o h d -> (b o) (h d)"), VST[:, :]).then_inc(kv_out, 16)
            pool.wait_ge(sb_out, SB_PAIRS)
            pool.wait_ge(sb_tail, SB_ITEMS)
            pool.wait_ge(tok_tr, NTOK)
            link(g.memset(BD[:, :], GLA_SCALE))
            bd3 = BD[:, :].rearrange("p (a b) -> p a b", b=SUB)
            link(g.affine_select(out=bd3, in_=bd3, compare_op=ALU.is_ge, fill=0.0, base=0,
                                 pattern=[[-SUB, P // SUB], [0, SUB]], channel_multiplier=1))
            link(g.affine_select(out=bd3, in_=bd3, compare_op=ALU.is_ge, fill=0.0, base=SUB - 1,
                                 pattern=[[SUB, P // SUB], [0, SUB]], channel_multiplier=-1))
            link(g.memset(ZSEL[:, :], 0.0))
            g.memset(ZSEL[:, :].rearrange("p (a b) -> p a b", b=SUB)[:, :, SUB - 1:SUB], 1.0).then_inc(consts, 1)
            def state_load(h):
                pool.dma_start(SS[:, h % 2, :, :], state_gla[0, :, h].rearrange("b k v -> k b v"))\
                    .then_inc(state_in[h % 2], 16)
            pool.wait_ge(kv_out, 16 * 4)
            state_load(0)
            state_load(1)
            for h in range(GH):
                if h >= 1:
                    pool.wait_ge(dec_mm, (h - 1) * NEV + PAIRS)
                g.tensor_tensor(KM[:, :, :], KGS[:, h * DK:(h + 1) * DK].unsqueeze(1).to_broadcast([TS, TS, DK]),
                                ident[0:TS, 0:TS].unsqueeze(2).to_broadcast([TS, TS, DK]), ALU.mult)\
                    .then_inc(km_ready, 1)
                pool.wait_ge(dec_taken, h * NEV + PAIRS)
                pool.dma_start(new_state_sample[0, :, h].rearrange("b k v -> k b v"), SS[:, h % 2, :, :])\
                    .then_inc(state_out[h % 2], 16)
                if h + 2 < GH:
                    pool.wait_ge(state_out[h % 2], 16)
                    pool.wait_ge(dec_mm, (h + 1) * NEV)
                    state_load(h + 2)
            pool.wait_ge(g_stev, 2)
            pool.dma_start(new_state_prompt[0, 0].rearrange("h k v -> k h v"), SFIN).then_inc(g_stout, 16)
            pool.wait_ge(kv_outb, 16 * TB)
            pool.wait_ge(kv_out, 16 * (TB + 2))
            pool.wait_ge(g_stout, 16)
            for s in range(2):
                pool.wait_ge(state_out[s], 32)

        @block.scalar
        def _(act):
            link = linker(act, act_own)
            s = nc.scalar
            act.wait_ge(tr_done, 1)
            s.activation(CE[:, :], ps[:, 7, 0:KC * NC], ACT.Exp, scale=-1.0).then_inc(silu_c, 1)
            for k in range(0, KC, 2):
                act.wait_ge(tr_done, 3 + k)
                s.activation(X[:, k, :], ps[:, k % 4, 0:T], ACT.Copy).then_inc(x_act, 1)

            def rs(dst, var, n):
                act.wait_ge(var_ready, n)
                link(s.activation(dst, var, ACT.Ln))
                s.activation(dst, dst, ACT.Exp, scale=-0.5).then_inc(rs_ready, 1)

            rs(rstd[:, :], rvar[:, :], 1)

            def mod_row(done, count, ready, bank=4):
                act.wait_ge(done, count)
                s.activation(MROW[:, :], ps[:, bank, :], ACT.Copy).then_inc(ready, 1)

            def h_high(n0, before=None):
                for q in range(4):
                    if before is not None:
                        before(q)
                    act.wait_ge(h32_ready, n0 + q + 1)
                    s.activation(H_HI[:, 4 * q:4 * q + 4, :], F_LO[:, 4 * q:4 * q + 4, :], ACT.Copy)\
                        .then_inc(hhi_ready, 1)

            def hi(n, j, first=False):
                act.wait_ge(raw_in[j], n[0])
                if not first:
                    act.wait_ge(unit_used, n[1])
                s.activation(HI[:, j, :], RAW[:, j, :], ACT.Copy).then_inc(hi_ready, 1)

            def hi_n(nb, u, first=False):
                hi((nb * 4 + (64 // 4 * (u // 4) + 16), nb + (u - 3)), u % 4, first)

            def evac(dst, m, wait_val, used_val):
                if m < 3:
                    act.wait_ge(bank_done, wait_val)
                else:
                    act.wait_ge(unit_used, used_val)
                s.activation(dst, ps[:, m, 0:T], ACT.Copy).then_inc(bank_out, 1)

            with act.Fori(0, NMA) as g:
                mod_row(ad4_used, g * 4 + 4, modrow_a)

            h_high(0, lambda q: hi((16, 0), q, True))
            for u in range(4, 8):
                hi_n(0, u)
            act.wait_ge(misc_in, 64)
            s.activation(WGH[:, :, :], WG[:, :, :], ACT.Copy).then_inc(wg_split, 1)

            def group(g, w0, bank0, dst0, adag, row=None, par=None):
                for u in range(3):
                    hi_n(g * UPC + w0, u)
                for m in range(MT):
                    evac(PROJ[:, bass.ds(g * MT + (dst0 - MT + m), 1), :].rearrange("p o t -> p (o t)"), m,
                         g * 3 + (bank0 - 3 + m + 1), g * UPC + w0)
                if adag is not None:
                    mod_row(ada_used, g * 4 + adag, modrow_b)
                for u in range(3, UPC):
                    hi_n(g * UPC + w0, u)
                    if u == 5 and row is not None:
                        act.wait_ge(qb_mm, row + 1)
                        if not (isinstance(row, int) and row < 2):
                            act.wait_ge(kpage_used, row * PAGES - PAGES)
                        for half in range(2):
                            ins = s.activation(QBC[:, par, half * 512:half * 512 + 512], ps[:, 6 + half, :], ACT.Copy)
                        ins.then_inc(qb_ready, 1)

            with act.Fori(1, DOT0 - 1) as g:
                group(g, 0, 0, 0, 0)
            group(DOT0 - 1, 0, 0, 0, 0, 0, 0)
            with act.Fori(0, (NMB - DOT0) // 2) as b2:
                group(b2 * 2 + DOT0, 0, 0, 0, 0, b2 * 2 + 1, 1)
                group(b2 * 2 + (DOT0 + 1), 0, 0, 0, 0, b2 * 2 + 2, 0)
            for g in range(NMB, NIN - 1):
                row = g - DOT0 + 1
                group(g, 0, 0, 0, 0 if g == NMB else None, row, row % 2)
            group(NIN - 1, 0, 0, 0, None)
            for m in range(MT):
                evac(PROJ[:, (NIN - 1) * MT + m, :], m, NIN * 3 - 3 + m + 1, NIN * UPC)
            act.wait_ge(glow_mm, 1)
            s.activation(GLOW[:, :], ps[0:RANK, 6, 0:T], ACT.Copy).then_inc(glow_ready, 1)

            act.wait_ge(consts, 3)
            for j, (chunks, t0, nt, dst) in enumerate(tok_jobs):
                if j % 2 == 0:
                    act.wait_ge(tok_tr, j + 1)
                    s.activation(dst, ps[0:nt, j % 4, :], ACT.Copy).then_inc(tok_act, 1)
            def probs(k):
                act.wait_ge(sb_arg, k + 1)
                if k < SB_PAIRS:
                    s.activation(SA[:, k % 2, :, :], SA[:, k % 2, :, :], ACT.Exp).then_inc(sb_a, 1)
                else:
                    s.activation(AD[:, :, :].rearrange("p b n -> p (b n)"), dec_view(SE), ACT.Exp).then_inc(d_a, 1)

            def exp_log(k):
                act.wait_ge(sb_abs, k + 1)
                e, a = (SE[:, k % 2, :, :], SA[:, k % 2, :, :]) if k < SB_PAIRS else (dec_view(SE), dec_view(SA))
                link(s.activation(e, a, ACT.Exp, scale=-1.0))
                s.activation(a, e, ACT.Ln, bias=1.0).then_inc(sb_ln, 1)

            def sb_result(k):
                act.wait_ge(sb_o, k + 1)
                s.activation(PROJ[:, C_Q + 2 * k:C_Q + 2 * k + 2, 0:TP],
                             ps[:, 4, :].rearrange("p (e t) -> p e t", e=2), ACT.Copy).then_inc(sb_out, 1)

            for slot in range(SB_ITEMS + 1):
                if slot >= 2:
                    probs(slot - 2)
                if slot < SB_ITEMS:
                    exp_log(slot)
                if slot >= 2:
                    sb_result(slot - 2)
                if 1 <= slot <= NMC:
                    mod_row(adc_used, 4 * slot, modrow_c, 5)

            def v_out(b):
                act.wait_ge(vpage_used, PAGES * (b + 1))
                if b >= 1:
                    act.wait_ge(v_sel, b)
                s.activation(DOUT[:, 0:512], ps[:, 4, :], ACT.Copy)
                s.activation(DOUT[:, 512:1024], ps[:, 5, :], ACT.Copy).then_inc(v_evac, 1)

            def gate_exp(c):
                if c >= 2:
                    act.wait_ge(silu_r, c - 1)
                s.activation(RT[:, c % 2, :], SIL[:, c, :], ACT.Exp, scale=-1.0).then_inc(r_exp, 1)

            act.wait_ge(g_abs, 1)
            act.wait_ge(sb_z, SB_PAIRS)
            link(s.activation(GE[:, :, :], GL[:, :, :], ACT.Exp, scale=-1.0))
            s.activation(GL[:, :, :], GE[:, :, :], ACT.Ln, bias=1.0).then_inc(g_ln, 1)
            probs(SB_PAIRS)
            act.wait_ge(g_cum, 1)
            s.activation(ALP[:, :, :], GATE[:, :, TP:T], ACT.Exp, scale=-1.0 / 16).then_inc(alp_ready, 1)
            s.activation(QT[:, :, :], CB1[:, :, :], ACT.Exp, scale=-1.0 / 16).then_inc(g_eq, 1)
            for i in range(1, NSUB + 1):
                act.wait_ge(g_kdiff, i)
                s.activation(kview(i), kview(i), ACT.Exp, scale=1.0 / 16).then_inc(g_kexp, 1)
                if i in SILU_TICK:
                    gate_exp(SILU_TICK[i])
                if i - 3 in V_TICK:
                    v_out(V_TICK[i - 3])
            for t in range(SUB):
                act.wait_ge(g_ddiff, t + 1)
                s.activation(dview(t), dview(t), ACT.Exp, scale=-1.0 / 16).then_inc(g_dexp, 1)
                if t < 2:
                    act.wait_ge(g_kft, t + 1)
                    s.activation(KFT[:, t * 512:t * 512 + 512], ps[:, 2 + t, :], ACT.Copy).then_inc(g_kftev, 1)
                elif t < 4:
                    act.wait_ge(g_st, t - 1)
                    s.activation(SFIN[:, 2 * (t - 2):2 * (t - 2) + 2, :].rearrange("p h v -> p (h v)"),
                                 ps[:, t, :], ACT.Copy).then_inc(g_stev, 1)
                if NSUB + t - 2 in V_TICK:
                    v_out(V_TICK[NSUB + t - 2])
            for h in range(GH):
                act.wait_ge(g_o, h + 1)
                s.activation(PROJ[:, KC // 2 + VD * h:KC // 2 + VD * h + VD, 0:TP],
                             ps[:, 2 + h % 2, :].rearrange("p (v t) -> p v t", v=VD), ACT.Copy).then_inc(g_oev, 1)

            for st in range(2):
                act.wait_ge(state_out[st], 32)
            act.wait_ge(g_stout, 16)
            for u in range(4):
                hi_n(W_OUT, u)

            rs(rstd[0:NRM, :], rvar[0:NRM, :], 2)
            act.wait_ge(norm_bc, 1)
            s.activation(MIXR[:, :, :], ps[:, 4:4 + GH, 0:T], ACT.Copy).then_inc(norm_sb, 1)
            h_high(4)
            for u in range(4, 8):
                hi_n(W_OUT, u)
            B1 = NIN * 3
            with act.Fori(1, NOUT) as g:
                group(g, W_OUT, B1, KC, NMB * 4)
            for m in range(MT):
                evac(PROJ[:, KC + (NOUT - 1) * MT + m, :], m, B1 + NOUT * 3 - 3 + m + 1, W_OUT + NOUT * UPC)
            mod_row(ada_used, (NMB + NOUT) * 4, modrow_b)
            for u in range(4):
                hi_n(W_FFN, u)
            rs(rstd[:, :], rvar[:, :], 3)
            for q in range(4):
                act.wait_ge(x_new, q + 1)
                s.activation(SQD[:, 4 * q:4 * q + 4, :], X[:, 4 * q:4 * q + 4, :], ACT.Square).then_inc(sq_ready, 1)
            rs(rstd[:, :], rvar[:, :], 4)

            def glu_exp(g):
                act.wait_ge(unit_used, g * 2 * UPC + (W_FFN + UPC))
                s.activation(GLU[:, :, :], ps[:, 0:MT, 0:T], ACT.Exp, scale=-1.0).then_inc(glu_e, 1)

            def glu_high(g):
                act.wait_ge(glu_step, g * NGS + NGS)
                s.activation(A_HI[:, bass.ds(g * MT, MT), :], GLU[:, :, :], ACT.Copy).then_inc(glu_hi, 1)

            def ffn(g, prev):
                for u in range(3):
                    hi_n(g * 2 * UPC + W_FFN, u)
                if prev is not None:
                    glu_high(prev)
                for u in range(3, UPC + 3):
                    hi_n(g * 2 * UPC + W_FFN, u)
                if prev is not None:
                    act.wait_ge(glu_done, prev + 1)
                glu_exp(g)
                for u in range(UPC + 3, 2 * UPC):
                    hi_n(g * 2 * UPC + W_FFN, u)

            h_high(8)
            for u in range(4, UPC + 3):
                hi_n(W_FFN, u)
            glu_exp(0)
            for u in range(UPC + 3, 2 * UPC):
                hi_n(W_FFN, u)
            with act.Fori(1, NFF) as g:
                ffn(g, g - 1)

            def down4(nb, mid=None):
                for u in range(4):
                    if u == 3 and mid:
                        mid()
                    hi_n(nb, u)

            down4(W_DOWN, lambda: glu_high(NFF - 1))
            with act.Fori(1, FC // 4) as j:
                down4(j * 4 + W_DOWN)
            BD0 = (NIN + NOUT) * 3

            def down_out(half):
                for m in range(8):
                    if m < 7:
                        act.wait_ge(bank_done, BD0 + half * 7 + m + 1)
                    else:
                        act.wait_ge(unit_used, W_DOWN + (half + 1) * FC)
                    s.activation(F_HI[:, half * 8 + m, :], ps[:, m, 0:T], ACT.Copy).then_inc(bank_out, 1)

            down4(W_DOWN + FC, lambda: down_out(0))
            with act.Fori(1, FC // 4) as j:
                down4(j * 4 + (W_DOWN + FC))
            down_out(1)
            rs(rstd[:, :], rvar[:, :], 5)

            n = 0
            for q in range(4):
                for t0, nt, dst in y_jobs:
                    act.wait_ge(y_tr, n + 1)
                    s.activation(dst(q), ps[0:nt, 2 + n % 4, :], ACT.Copy).then_inc(y_rows, 1)
                    n += 1

        @block.vector
        def _(dve):
            link = linker(dve, dve_own)
            v = nc.vector
            link(v.memset(CTK[:, :, :], 0.0))
            dve.wait_ge(silu_c, 1)
            link(v.tensor_scalar(CE[:, :], CE[:, :], 1.0, None, ALU.add))
            link(v.reciprocal(CE[:, :], CE[:, :]))
            v.tensor_tensor(CTK[:, :, 0:NC], ps[:, 7, 0:KC * NC].rearrange("p (k t) -> p k t", k=KC),
                            CE[:, :].rearrange("p (k t) -> p k t", k=KC), ALU.mult).then_inc(ct_ready, 1)
            dve.wait_ge(tr_done, 2)
            v.tensor_copy(vec1[:, :], ps[:, 5, 0:NMOD + KC]).then_inc(vec_ready, 1)
            v.tensor_copy(vec2[:, 0:NV2], ps[:, 5, 128:128 + NV2]).then_inc(vec_ready, 1)
            for k in range(1, KC, 2):
                dve.wait_ge(tr_done, 3 + k)
                v.tensor_copy(X[:, k, :], ps[:, k % 4, 0:T]).then_inc(x_dve, 1)
            dve.wait_ge(x_act, KC // 2)
            dve.wait_ge(x_dve, KC // 2)
            for q in range(4):
                xq = X[:, 4 * q:4 * q + 4, :]
                v.tensor_tensor(F_LO[:, 4 * q:4 * q + 4, :], xq, xq, ALU.mult).then_inc(sq_ready, 1)

            def rstd_of(dst, var, src, width, n, done=None):
                v.tensor_scalar(var, src, 1.0 / width, EPS, ALU.mult, ALU.add).then_inc(var_ready, 1)
                dve.wait_ge(rs_ready, n)
                link(v.tensor_tensor(var, var, dst, ALU.mult))
                link(v.tensor_tensor(var, var, dst, ALU.mult))
                link(v.tensor_scalar(var, var, -0.5, 1.5, ALU.mult, ALU.add))
                if done is None:
                    link(v.tensor_tensor(dst, dst, var, ALU.mult))
                else:
                    v.tensor_tensor(dst, dst, var, ALU.mult).then_inc(done, 1)

            dve.wait_ge(sums_done, 1)
            rstd_of(rstd[:, :], rvar[:, :], ps[:, 6, 0:T], D, 1)
            dve.wait_ge(vec_ready, 2)

            def mod_col(made, count, g, ready, bank=5):
                dve.wait_ge(made, count)
                v.tensor_tensor(MOD[:, bass.ds(g * 4, 4), :],
                                ps[:, bank, 0:4 * NC].rearrange("p (m t) -> p m t", m=4),
                                vec1[:, bass.ds(g * 4, 4)].unsqueeze(2).to_broadcast([P, 4, NC]), ALU.add)\
                    .then_inc(ready, 1)


            def low_h(n0, q):
                cs = slice(4 * q, 4 * q + 4)
                dve.wait_ge(hhi_ready, n0 + q + 1)
                v.tensor_tensor(H_LO[:, cs, :], F_LO[:, cs, :], H_HI[:, cs, :].bitcast(F32), ALU.subtract)\
                    .then_inc(h_ready, 1)

            def x_norm(q):
                cs = slice(4 * q, 4 * q + 4)
                link(v.tensor_tensor(F_LO[:, cs, :], X[:, cs, :], rstd[:, :].unsqueeze(1).to_broadcast([P, 4, T]),
                                     ALU.mult))

            def build_h(gain, shift, scl, n0, normed=False, between=None):
                link(v.scalar_tensor_tensor(scale_t[:, :, :], MOD[:, scl:scl + KC, :], 1.0,
                                            gain.unsqueeze(2).to_broadcast([P, KC, NC]), ALU.add, ALU.mult))
                for q in range(4):
                    cs = slice(4 * q, 4 * q + 4)
                    if not normed:
                        x_norm(q)
                    link(v.tensor_tensor(F_LO[:, cs, TP:T], F_LO[:, cs, TP:T], scale_t[:, cs, 1:NC], ALU.mult))
                    v.tensor_tensor(F_LO[:, cs, TP:T], F_LO[:, cs, TP:T],
                                    MOD[:, shift + 4 * q:shift + 4 * q + 4, 1:NC], ALU.add)
                    for k in range(4 * q, 4 * q + 4):
                        ins = v.tensor_scalar(F_LO[:, k, 0:TP], F_LO[:, k, 0:TP], scale_t[:, k, 0:1],
                                              MOD[:, shift + k, 0:1], ALU.mult, ALU.add)
                    ins.then_inc(h32_ready, 1)
                    if between is not None:
                        between(q)
                    if q >= 1:
                        low_h(n0, q - 1)
                low_h(n0, 3)

            def lo(nb, u):
                dve.wait_ge(hi_ready, nb + (u + 1))
                v.tensor_tensor(LO[:, u % 4, :], RAW[:, u % 4, :], HI[:, u % 4, :].bitcast(F32), ALU.subtract)\
                    .then_inc(lo_ready, 1)

            for q in range(4):
                x_norm(q)
            with dve.Fori(0, NMA) as g:
                mod_col(modt_a, g + 1, g, mod_a)
            dve.wait_ge(mod_a, NMA)
            build_h(vec1[:, NMOD:NMOD + KC], 0, KC, 0, True, lambda q: lo(0, q))
            for u in range(4, UPC):
                lo(0, u)
            dve.wait_ge(wg_split, 1)
            v.tensor_tensor(WGL[:, :, :], WG[:, :, :], WGH[:, :, :].bitcast(F32), ALU.subtract).then_inc(wg_split, 1)

            def in_group(g, b=None, par=None, nxt=None, mod=True):
                for u in range(UPC):
                    if u == UPC - 1 and mod:
                        mod_col(modt_b, g, g + (NMA - 1), mod_b)
                    lo(g * UPC, u)
                    if u == 0 and nxt is not None:
                        v.tensor_copy(QB[:, nxt[1], :].unsqueeze(2), PROJ[:, C_Q:C_Q + H, bass.ds(nxt[0] + TP, 1)])\
                            .then_inc(q_col, 1)
                    if b is not None:
                        if u == 0:
                            dve.wait_ge(qb_ready, b + 1)
                        dve.wait_ge(kpage_in[u % 4], b * 32 + (u // 4 * 16 + 16))
                        for h in range(H):
                            kp = KP[:, u % 4, h * DH:(h + 1) * DH]
                            ins = v.tensor_tensor_reduce(kp, kp, QBC[:, par, h * DH:(h + 1) * DH], 1.0, 0.0,
                                                         ALU.mult, ALU.add, ZS[:, u * H + h:u * H + h + 1])
                        ins.then_inc(kpage_used, 1)
                if b is not None:
                    dve.wait_ge(kpage_used, b * PAGES + PAGES)
                    v.tensor_copy(ZD[:, bass.ds(b, 1), :].rearrange("p o n -> p (o n)"), ZS[:, :]).then_inc(zs_taken, 1)
                    dve.wait_ge(zs_taken, b + 1)

            with dve.Fori(1, DOT0 - 1) as g:
                in_group(g)
            dve.wait_ge(bank_out, 2 * MT)
            in_group(DOT0 - 1, nxt=(0, 0))
            with dve.Fori(0, (NMB - DOT0) // 2) as b2:
                in_group(b2 * 2 + DOT0, b2 * 2, 0, (b2 * 2 + 1, 1))
                in_group(b2 * 2 + (DOT0 + 1), b2 * 2 + 1, 1, (b2 * 2 + 2, 0))
            for g in range(NMB, NIN - 1):
                b = g - DOT0
                in_group(g, b, b % 2, (b + 1, (b + 1) % 2), mod=(g == NMB))
            in_group(NIN - 1, TS - 1, 1, mod=False)

            dve.wait_ge(consts, 3)
            for j, (chunks, t0, nt, dst) in enumerate(tok_jobs):
                if j % 2:
                    dve.wait_ge(tok_tr, j + 1)
                    v.tensor_copy(dst, ps[0:nt, j % 4, :]).then_inc(tok_dve, 1)

            def softplus_tail(e, l, z, t, out, chain):
                chain(v.tensor_scalar(t, e, 1.0, None, ALU.add))
                chain(v.scalar_tensor_tensor(t, t, 1.0, e, ALU.subtract, ALU.subtract))
                chain(v.tensor_tensor(t, l, t, ALU.subtract))
                chain(v.scalar_tensor_tensor(out, z, 0.0, t, ALU.max, ALU.add))

            zd = ZD[:, :, :].rearrange("p b n -> p (b n)")

            def scores(k):
                if k < SB_PAIRS:
                    dve.wait_ge(sb_z, k + 1)
                    if k >= 2:
                        dve.wait_ge(sb_o, k - 1)
                    z, a = ZB[:, k % 2, :, :], SA[:, k % 2, :, :]
                    for e in range(2):
                        link(v.tensor_scalar(ZB[:, k % 2, e, :], ps[:, e, 0:384], SB_SCALE,
                                             bias_h[:, 2 * k + e:2 * k + e + 1], ALU.mult, ALU.add))
                else:
                    dve.wait_ge(sb_o, k - 1)
                    z, a = dec_view(ZB), dec_view(SA)
                    link(v.scalar_tensor_tensor(z.rearrange("p (n h) -> p n h", h=H),
                                                zd.rearrange("p (n h) -> p n h", h=H), SB_SCALE,
                                                bias_h[:, :].unsqueeze(1).to_broadcast([P, TS * PAGES, H]),
                                                ALU.mult, ALU.add))
                v.scalar_tensor_tensor(a, z, -1.0, z, ALU.mult, ALU.max).then_inc(sb_abs, 1)

            def softplus(k):
                dve.wait_ge(sb_ln, k + 1)
                if k < SB_PAIRS:
                    sp_ = SP[:, k % 2, :, :]
                    softplus_tail(SE[:, k % 2, :, :], SA[:, k % 2, :, :], ZB[:, k % 2, :, :], sp_, sp_, link)
                    v.tensor_tensor(sp_, sp_, M01[:, :].unsqueeze(1).to_broadcast([P, 2, 384]), ALU.mult)\
                        .then_inc(sb_sp, 1)
                else:
                    spd = dec_view(SP)
                    softplus_tail(dec_view(SE), dec_view(SA), dec_view(ZB), spd, spd, link)
                    zp = spd.rearrange("p (b g h) -> p b g h", b=TS, g=PAGES)
                    link(v.memset(DR[:, :, PAGES - 1, :], 0.0))
                    for pg in range(PAGES - 2, -1, -1):
                        ins = v.tensor_tensor(DR[:, :, pg, :], DR[:, :, pg + 1, :], zp[:, :, pg + 1, :], ALU.add)
                        if pg:
                            link(ins)
                    ins.then_inc(sb_sp, 1)

            def log_probs(k):
                dve.wait_ge(sb_tail, k + 1)
                if k < SB_PAIRS:
                    a = SA[:, k % 2, :, :]
                    link(v.tensor_tensor(a, ZB[:, k % 2, :, :], ps[:, 2:4, 0:384], ALU.subtract))
                    v.scalar_tensor_tensor(a, a, 0.0, MNEG[:, :].unsqueeze(1).to_broadcast([P, 2, 384]),
                                           ALU.min, ALU.add).then_inc(sb_arg, 1)
                else:
                    a = dec_view(SE)
                    link(v.tensor_tensor(a, dec_view(ZB), ps[:, 2, :], ALU.subtract))
                    v.tensor_scalar(a, a, 0.0, None, ALU.min).then_inc(sb_arg, 1)

            for slot in range(SB_ITEMS + 1):
                if slot >= 2:
                    log_probs(slot - 2)
                if 1 <= slot:
                    softplus(slot - 1)
                if slot < SB_ITEMS:
                    scores(slot)
                if 2 <= slot <= NMC + 1:
                    mod_col(modt_c, slot - 1, NMA + NMB + slot - 2, mod_c, 6)

            for h in range(GH):
                dve.wait_ge(g_mm, h + 1)
                link(v.tensor_scalar(GATE[:, h, :], ps[:, 4 + h, 0:T], vec2[:, V2["b_gate"] + h:V2["b_gate"] + h + 1], -1.0,
                                     ALU.add, ALU.mult))
            v.scalar_tensor_tensor(GL[:, :, :], GATE[:, :, :], -1.0, GATE[:, :, :], ALU.mult, ALU.max).then_inc(g_abs, 1)
            log_probs(SB_PAIRS)
            dve.wait_ge(g_ln, 1)
            softplus_tail(GE[:, :, :], GL[:, :, :], GATE[:, :, :], GT[:, :, :], GATE[:, :, :], link)
            dve.wait_ge(d_a, 1)
            dve.wait_ge(sb_o, SB_PAIRS)
            def blocks(t):
                return t[:, :, 0:TP].rearrange("p h (b n) -> p h b n", n=SUB)
            src, dst = GATE, CB0
            for k in (1, 2, 4, 8):
                link(v.tensor_tensor(blocks(dst)[:, :, :, k:], blocks(src)[:, :, :, k:],
                                     blocks(src)[:, :, :, 0:SUB - k], ALU.add))
                link(v.tensor_copy(blocks(dst)[:, :, :, 0:k], blocks(src)[:, :, :, 0:k]))
                src, dst = dst, (CB1 if dst is CB0 else CB0)
            link(v.memset(BX[:, :, 0:1], 0.0))
            for i in range(NSUB):
                link(v.tensor_tensor(BX[:, :, i + 1:i + 2], BX[:, :, i:i + 1],
                                     CB1[:, :, i * SUB + SUB - 1:i * SUB + SUB], ALU.add))
            v.tensor_tensor(blocks(CAB), blocks(CB1), BX[:, :, 0:NSUB].unsqueeze(3).to_broadcast([P, GH, NSUB, SUB]),
                            ALU.add).then_inc(g_cum, 1)
            dve.wait_ge(consts, 4)
            v.tensor_scalar(QS[:, :, :], PROJ[:, C_GQ:C_GQ + GH, TP:T], GLA_SCALE, None, ALU.mult).then_inc(alp_ready, 1)
            dve.wait_ge(g_eq, 1)
            v.scalar_tensor_tensor(QT[:, :, :], PROJ[:, C_GQ:C_GQ + GH, 0:TP], GLA_SCALE, QT[:, :, :],
                                   ALU.mult, ALU.mult).then_inc(g_qt, 1)
            for h in range(GH):
                v.memset(ps[:, h, 0:384], 0.0).then_inc(g_qt, 1)
            dve.wait_ge(g_cum, 1)

            def put_row(b):
                dve.wait_ge(v_sel, b + 1)
                v.tensor_copy(PROJ[:, 0:H, TP + b:TP + b + 1], ps[:, 6, 0:H].unsqueeze(2)).then_inc(v_put, 1)

            def kdiff(i):
                if i > DEEP:
                    dve.wait_ge(g_off, i - DEEP)
                v.tensor_tensor(kview(i), CAB[:, :, 0:SUB * i], BX[:, :, i:i + 1].to_broadcast([P, GH, SUB * i]),
                                ALU.subtract).then_inc(g_kdiff, 1)

            def dec_take(n):
                h, j = divmod(n, NEV)
                dve.wait_ge(dec_mm, n + 1)
                if j < PAIRS:
                    if j == 0:
                        dve.wait_ge(state_in[h % 2], 16 * (h // 2 + 1))
                    for e in range(2):
                        st = SS[:, h % 2, 2 * j + e, :]
                        ins = v.scalar_tensor_tensor(st, st, ALP[:, h, 2 * j + e:2 * j + e + 1],
                                                     ps[:, 7, e * DV:(e + 1) * DV], ALU.mult, ALU.add)
                else:
                    ins = v.tensor_copy(DO[:, h, :], ps[:, 7, 0:VD * TS])
                ins.then_inc(dec_taken, 1)

            def silu_chunk(c):
                dve.wait_ge(r_exp, c + 1)
                rt = RT[:, c % 2, :]
                link(v.tensor_scalar(rt, rt, 1.0, None, ALU.add))
                link(v.reciprocal(rt, rt))
                v.tensor_tensor(SIL[:, c, :], SIL[:, c, :], rt, ALU.mult).then_inc(silu_r, 1)

            def take(i):
                if i - LAG in V_TICK and V_TICK[i - LAG] >= 1:
                    put_row(V_TICK[i - LAG] - 1)
                if i - LAG in DEC_TICK:
                    dec_take(DEC_TICK[i - LAG])

            dve.wait_ge(alp_ready, 2)
            kdiff(1)
            for i in range(1, NSUB + 1):
                if i < NSUB:
                    kdiff(i + 1)
                dve.wait_ge(g_kexp, i)
                v.tensor_tensor(kview(i), kview(i), PROJ[:, C_GK:C_GK + GH, 0:SUB * i], ALU.mult).then_inc(g_kd, 1)
                take(i)
                if i - 1 in SILU_TICK:
                    silu_chunk(SILU_TICK[i - 1])
            dve.wait_ge(g_off, NSUB - 1)
            for h in range(GH):
                v.tensor_copy(ATT[:, h, :, :].rearrange("p a b -> p (a b)"), ps[:, h, 0:384]).then_inc(g_offev, 1)

            def in_blocks(c0, a, b):
                return PROJ[:, c0:c0 + GH, 0:TP].rearrange("p h (b n) -> p h b n", n=SUB)[:, :, :, a:b]

            def d4(t):
                return dview(t).rearrange("p (h b) n -> p h b n", h=GH)

            cb = CB1[:, :, :].rearrange("p h (b n) -> p (h b) n", n=SUB)

            def ddiff(t):
                if t >= DEEP:
                    dve.wait_ge(g_diag, t - DEEP + 1)
                v.tensor_tensor(dview(t), cb[:, :, t:SUB], cb[:, :, t:t + 1].to_broadcast([P, GH * NSUB, SUB - t]),
                                ALU.subtract).then_inc(g_ddiff, 1)

            ddiff(0)
            for t in range(SUB):
                if t + 1 < SUB:
                    ddiff(t + 1)
                dve.wait_ge(g_dexp, t + 1)
                link(v.tensor_tensor(d4(t), d4(t), in_blocks(C_GQ, t, SUB), ALU.mult))
                v.tensor_tensor(d4(t), d4(t), in_blocks(C_GK, t, t + 1).to_broadcast([P, GH, NSUB, SUB - t]),
                                ALU.mult).then_inc(g_dprod, 1)
                take(NSUB + 1 + t)
            dve.wait_ge(g_diag, SUB)
            dve.wait_ge(g_offev, GH)
            for i in range(2 * NSUB + 1, 2 * NSUB + 1 + LAG):
                take(i)
            diag_t = DIAG_T[:, :].rearrange("p (a b) -> p a b", a=2)
            for h in range(GH):
                link(v.tensor_tensor(diag_t, ps[:, h // 2, (h % 2) * TP:(h % 2) * TP + TP].rearrange("p (a b) -> p a b", a=2),
                                     BD[:, :].unsqueeze(1).to_broadcast([P, 2, P]), ALU.mult))
                v.tensor_tensor(ATT[:, h, 0:3:2, :], ATT[:, h, 0:3:2, :], diag_t, ALU.add).then_inc(g_att, 1)
                dve.wait_ge(g_att, h + 1)

            put_row(TS - 1)

            def squares(q):
                mq = MIX[:, 4 * q:4 * q + 4, :]
                v.tensor_tensor(F_LO[:, 4 * q:4 * q + 4, :], mq, mq, ALU.mult).then_inc(msq, 1)

            dve.wait_ge(v_put, TS)
            dve.wait_ge(sb_out, SB_PAIRS)
            squares(0)
            squares(1)
            dve.wait_ge(dec_taken, GH * NEV)
            dve.wait_ge(g_oev, GH)
            link(v.tensor_copy(MIX[:, H:KC, TP:T], DO[:, :, :].rearrange("p h (v b) -> p (h v) b", v=VD)))
            squares(2)
            squares(3)
            for u in range(4):
                lo(W_OUT, u)
            dve.wait_ge(msum, 1)
            rstd_of(rstd[0:NRM, :], rvar[0:NRM, :], ps[0:NRM, 4, 0:T], 1, 2, done=rs12_ready)
            dve.wait_ge(silu_r, GH * VD)
            for q in range(4):
                if q < 2:
                    cs = slice(4 * q, 4 * q + 4)
                    dve.wait_ge(norm_bc, 2 + q)
                    v.scalar_tensor_tensor(F_LO[:, cs, :], MIX[:, cs, :], vec2[:, V2["sb"]:V2["sb"] + 1],
                                           ps[:, 4 * q:4 * q + 4, 0:T], ALU.mult, ALU.mult).then_inc(h32_ready, 1)
                else:
                    dve.wait_ge(norm_sb, 1)
                    for vb in range(VD):
                        cs = slice(4 * q + vb, 4 * q + vb + 3, 2)
                        link(v.scalar_tensor_tensor(F_LO[:, cs, :], MIX[:, cs, :],
                                                    vec2[:, V2["gla"] + vb:V2["gla"] + vb + 1],
                                                    MIXR[:, 2 * (q - 2):2 * (q - 2) + 2, :], ALU.mult, ALU.mult))
                    cs = slice(4 * q, 4 * q + 4)
                    v.tensor_tensor(F_LO[:, cs, :], F_LO[:, cs, :], SIL[:, 4 * (q - 2):4 * (q - 2) + 4, :],
                                    ALU.mult).then_inc(h32_ready, 1)
                low_h(4, q)
                dve.wait_ge(h_ready, 4 + q + 1)

            def early_squares(src, squares, nch):
                link(v.tensor_tensor(squares[:, 0:nch, :], src[:, 0:nch, :], src[:, 0:nch, :], ALU.mult))
                while nch > 1:
                    half = nch // 2
                    ins = v.tensor_tensor(squares[:, 0:half, :], squares[:, 0:half, :],
                                          squares[:, nch - half:nch, :], ALU.add)
                    nch -= half
                    if nch > 1:
                        link(ins)
                ins.then_inc(sq_ready, 1)

            for u in range(4, UPC):
                lo(W_OUT, u)
            with dve.Fori(1, NOUT) as g:
                for u in range(7):
                    lo(g * UPC + W_OUT, u)
                mod_col(modt_b, g + NMB, g + (NMA + NMB + NMC - 1), mod_b)
                lo(g * UPC + W_OUT, 7)
            dve.wait_ge(bank_out, MT * (NIN + NOUT - 1))
            early_squares(MT_, SQD, KC - MT)
            mod_col(modt_b, NMB + NOUT, NMA + NMB + NMC + NOUT - 1, mod_b)

            def add_norm(src, gain, gate, squares, early, done, n, nr, nx, fill=None):
                for c in range(early, KC, 4):
                    dve.wait_ge(bank_out, n - KC + c + 4)
                    sq = src[:, c:c + 4, :]
                    v.tensor_tensor(squares[:, c:c + 4, :], sq, sq, ALU.mult).then_inc(sq_ready, 1)
                if fill is not None:
                    fill()
                link(v.tensor_tensor(scale_t[:, :, :], MOD[:, gate:gate + KC, :],
                                     gain.unsqueeze(2).to_broadcast([P, KC, NC]), ALU.mult))
                dve.wait_ge(sums_done, done)
                rstd_of(rstd[:, :], rvar[:, :], ps[:, 6, 0:T], D, nr)
                for q in range(4):
                    cs = slice(4 * q, 4 * q + 4)
                    link(v.tensor_tensor(src[:, cs, :], src[:, cs, :], rstd[:, :].unsqueeze(1).to_broadcast([P, 4, T]),
                                         ALU.mult))
                    link(v.tensor_tensor(squares[:, cs, TP:T], src[:, cs, TP:T], scale_t[:, cs, 1:NC], ALU.mult))
                    v.tensor_tensor(X[:, cs, TP:T], X[:, cs, TP:T], squares[:, cs, TP:T], ALU.add)
                    for k in range(4 * q, 4 * q + 4):
                        ins = v.scalar_tensor_tensor(X[:, k, 0:TP], src[:, k, 0:TP], scale_t[:, k, 0:1], X[:, k, 0:TP],
                                                     ALU.mult, ALU.add)
                    ins.then_inc(x_new, 1)
                    dve.wait_ge(x_new, nx + q + 1)
                    yield q

            def first_ffn_units():
                for u in range(4):
                    lo(W_FFN, u)

            dve.wait_ge(mod_b, NMB + NOUT)
            dve.wait_ge(mod_c, NMC)
            for q in add_norm(MT_, vec2[:, V2["post_mix"]:V2["post_mix"] + KC], 2 * KC, SQD, KC - MT, 2,
                              4 * (NIN + NOUT), 3, 0, first_ffn_units):
                continue
            dve.wait_ge(sums_done, 3)
            rstd_of(rstd[:, :], rvar[:, :], ps[:, 7, 0:T], D, 4)
            build_h(vec2[:, V2["pre_ffn"]:V2["pre_ffn"] + KC], 3 * KC, 4 * KC, 8)

            def glu_gate(g, nb):
                dve.wait_ge(glu_e, g + 1)
                v.tensor_scalar(GLU[:, :, :], GLU[:, :, :], 1.0, None, ALU.add).then_inc(glu_step, 1)
                for m in range(MT):
                    lo(nb, UPC + 3 + m)
                    dve.wait_ge(glu_step, g * NGS + 1)
                    v.reciprocal(GLU[:, m, :], GLU[:, m, :]).then_inc(glu_step, 1)
                lo(nb, 2 * UPC - 1)
                dve.wait_ge(glu_step, g * NGS + MT + 1)
                v.tensor_tensor(GLU[:, :, :], GLU[:, :, :], ps[:, 0:MT, 0:T], ALU.mult).then_inc(glu_step, 1)

            def glu_up(g):
                dve.wait_ge(unit_used, g * (2 * UPC) + (W_FFN + 2 * UPC))
                dve.wait_ge(glu_step, g * NGS + MT + 2)
                v.tensor_tensor(GLU[:, :, :], GLU[:, :, :], ps[:, MT:2 * MT, 0:T], ALU.mult).then_inc(glu_step, 1)

            def glu_low(g):
                dve.wait_ge(glu_hi, g + 1)
                v.tensor_tensor(A_LO[:, bass.ds(g * MT, MT), :], GLU[:, :, :],
                                A_HI[:, bass.ds(g * MT, MT), :].bitcast(F32), ALU.subtract).then_inc(glu_done, 1)

            for u in range(4, UPC + 3):
                lo(W_FFN, u)
            glu_gate(0, W_FFN)
            with dve.Fori(1, NFF) as g:
                for u in range(3):
                    lo(g * (2 * UPC) + W_FFN, u)
                glu_up(g - 1)
                lo(g * (2 * UPC) + W_FFN, 3)
                glu_low(g - 1)
                for u in range(4, UPC + 3):
                    lo(g * (2 * UPC) + W_FFN, u)
                glu_gate(g, g * (2 * UPC) + W_FFN)
            for u in range(3):
                lo(W_DOWN, u)
            glu_up(NFF - 1)
            lo(W_DOWN, 3)
            glu_low(NFF - 1)
            with dve.Fori(1, FC // 4 + 1) as j:
                for u in range(4):
                    lo(j * 4 + W_DOWN, u)
            dve.wait_ge(bank_out, MT * (NIN + NOUT) + KC // 2)
            early_squares(F_HI, F_LO, KC // 2)
            with dve.Fori(FC // 4 + 1, 2 * FC // 4) as j:
                for u in range(4):
                    lo(j * 4 + W_DOWN, u)

            for q in add_norm(F_HI, vec2[:, V2["post_ffn"]:V2["post_ffn"] + KC], 5 * KC, F_LO, KC // 2, 4,
                              4 * (NIN + NOUT) + KC, 5, 4):
                continue

        @block.tensor
        def _(pe):
            mm = nc.tensor.matmul
            tr = nc.tensor.transpose
            pe.wait_ge(consts, 1)
            pe.wait_ge(c_in, 32)
            for k in range(KC):
                ins = tr(ps[:, 7, k * NC:(k + 1) * NC], CR[:, k * P:(k + 1) * P], ident[0:NC, 0:NC])
            ins.then_inc(tr_done, 1)
            pe.wait_ge(vec_in, 16 * 8)
            tr(ps[:, 5, 0:NMOD + KC], VR[0:NMOD + KC, 0, :], ident[0:NMOD + KC, 0:NMOD + KC])
            tr(ps[:, 5, 128:128 + NV2], VR[0:NV2, 1, :], ident[0:NV2, 0:NV2]).then_inc(tr_done, 1)
            pe.wait_ge(x_in, 16 * (TB + 1))
            for k in range(KC):
                if k >= 4:
                    pe.wait_ge(x_dve if k % 2 else x_act, (k - 4) // 2 + 1)
                for tb in range(TB):
                    tr(ps[:, k % 4, tb * P:(tb + 1) * P], XR[:, tb, k * P:(k + 1) * P], ident[:, :])
                tr(ps[:, k % 4, TP:T], XS[:, k * P:(k + 1) * P], ident[0:TS, 0:TS]).then_inc(tr_done, 1)

            def sums(src, bank, n0, done):
                for q in range(4):
                    pe.wait_ge(sq_ready, n0 + q + 1)
                    for k in range(4 * q, 4 * q + 4):
                        ins = mm(ps[:, bank, 0:T], ones[:, :], src[:, k, :], start=(k == 0), stop=(k == KC - 1))
                ins.then_inc(done, 1)

            def late_sums(src, n0, early):
                for i, k in enumerate([0] + list(range(early, KC))):
                    if i == 0 or (k - early) % 4 == 0:
                        n0 += 1
                        pe.wait_ge(sq_ready, n0)
                    ins = mm(ps[:, 6, 0:T], ones[:, :], src[:, k, :], start=(i == 0), stop=(k == KC - 1))
                ins.then_inc(sums_done, 1)

            def ada_block(ring, slot, a, bank=4):
                for j in range(4):
                    ins = mm(ps[32 * j:32 * j + 32, bank, :], CTK[:, 4 * a + j, :],
                             ring[:, slot, j * CG:(j + 1) * CG], start=(a == 0), stop=(a == 3))
                return ins

            def mod_turn(done, bank=5):
                for m in range(4):
                    ins = mm(ps[:, bank, m * NC:(m + 1) * NC], MROW[:, m * P:(m + 1) * P], sel_c[:, :],
                             start=True, stop=True)
                ins.then_inc(done, 1)

            def ada_group(g):
                for a in range(4):
                    pe.wait_ge(ad4_in[a], g * 16 + 16)
                    ada_block(AD4, a, a).then_inc(ad4_used, 1)

            pe.wait_ge(ct_ready, 1)
            ada_group(0)
            sums(F_LO, 6, 0, sums_done)
            pe.wait_ge(vec_ready, 2)
            pe.wait_ge(modrow_a, 1)
            mod_turn(modt_a)
            with pe.Fori(1, NMA) as g:
                ada_group(g)
                pe.wait_ge(modrow_a, g + 1)
                pe.wait_ge(mod_a, g)
                mod_turn(modt_a)

            def split_products(out, k, w_hi, w_lo, xh, xl, first, last):
                mm(out, w_hi, xh[:, k, :], start=first, stop=False)
                mm(out, w_hi, xl[:, k, :], start=False, stop=False)
                return mm(out, w_lo, xh[:, k, :], start=False, stop=last)

            def unit(u, nb, bank0, first, last, free=None, k0=None, done=None):
                pe.wait_ge(lo_ready, nb + (u + 1))
                s = u % 4
                for m in range(MT):
                    if first and free is not None:
                        free(m)
                    for kk in range(2):
                        cs = slice(kk * CG + m * P, kk * CG + (m + 1) * P)
                        ins = split_products(ps[:, bank0 + m, 0:T], 2 * u + kk if k0 is None else k0 + kk,
                                             HI[:, s, cs], LO[:, s, cs], H_HI, H_LO,
                                             first and kk == 0, last and kk == 1)
                    if last and done is not None and m < MT - 1:
                        ins.then_inc(done, 1)
                ins.then_inc(unit_used, 1)

            def group(g, w0, cg, row0, h0=None, free=None, q=None):
                for u in range(UPC):
                    if h0 is not None and u % 2 == 0:
                        pe.wait_ge(h_ready, h0 + u // 2 + 1)
                    unit(u, g * UPC + w0, 0, u == 0, u == UPC - 1, free, done=bank_done)
                    if u == 3 and row0 is not None:
                        pe.wait_ge(modrow_b, row0)
                        mod_turn(modt_b)
                    if u == 4 and q is not None:
                        pe.wait_ge(q_col, q[0] + 1)
                        if not isinstance(q[0], int) or q[0] > 0:
                            pe.wait_ge(qb_ready, q[0])
                        for h in range(H):
                            ins = mm(ps[:, 6 + h // 4, h % 4 * DH:h % 4 * DH + DH],
                                     QB[:, q[1], h:h + 1].to_broadcast([P, P]), ident[:, :], start=True, stop=True)
                        ins.then_inc(qb_mm, 1)
                    if u % 2 and cg is not None:
                        a = u // 2
                        pe.wait_ge(ada_in[a % 2], cg * 32 + (16 * (a // 2) + 16))
                        if a == 0 and row0 is not None:
                            pe.wait_ge(modrow_b, row0)
                        ada_block(ADA, a % 2, a).then_inc(ada_used, 1)

            pe.wait_ge(mod_a, NMA)
            group(0, 0, 0, None, 0, None)
            def in_group(g, q=None, cg=True, row0=True):
                group(g, 0, g if cg else None, g if row0 else None, None,
                      lambda m: pe.wait_ge(bank_out, g * MT + (m - MT + 1)), q)

            with pe.Fori(1, DOT0 - 1) as g:
                in_group(g)
            in_group(DOT0 - 1, (0, 0))
            with pe.Fori(0, (NMB - DOT0) // 2) as b2:
                in_group(b2 * 2 + DOT0, (b2 * 2 + 1, 1))
                in_group(b2 * 2 + (DOT0 + 1), (b2 * 2 + 2, 0))
            for g in range(NMB, NIN - 1):
                row = g - DOT0 + 1
                in_group(g, (row, row % 2), cg=False, row0=(g == NMB))
            in_group(NIN - 1, cg=False, row0=False)
            pe.wait_ge(wg_split, 2)
            pe.wait_ge(qb_ready, TS)
            for k in range(KC):
                ins = split_products(ps[0:RANK, 6, 0:T], k, WGH[:, k, :], WGL[:, k, :], H_HI, H_LO,
                                     k == 0, k == KC - 1)
            ins.then_inc(glow_mm, 1)

            def tok(j, job):
                chunks, t0, nt, dst = job
                for i, c in enumerate(chunks):
                    ins = tr(ps[0:nt, j % 4, i * P:(i + 1) * P], PROJ[:, c, t0:t0 + nt], ident[:, :])
                ins.then_inc(tok_tr, 1)

            pe.wait_ge(bank_out, NIN * MT)
            for j, job in enumerate(tok_jobs):
                if j >= 4:
                    pe.wait_ge(tok_dve if j % 2 else tok_act, (j - 4) // 2 + 1)
                tok(j, job)
            pe.wait_ge(tok_act, NTOK_ACT)
            pe.wait_ge(tok_dve, NTOK_DVE)
            pe.wait_ge(mod_b, NMB)
            pe.wait_ge(glow_ready, 1)
            pe.wait_ge(consts, 3)

            for slot in range(SB_ITEMS + 1):
                if 2 <= slot <= NMC + 1:
                    pe.wait_ge(modrow_c, slot - 1)
                    if slot > 2:
                        pe.wait_ge(mod_c, slot - 2)
                    mod_turn(modt_c, 6)
                if 1 <= slot <= NMC:
                    for a in range(4):
                        pe.wait_ge(adc_in[a], 16 * slot)
                        ada_block(ADC, a, a, 5).then_inc(adc_used, 1)
                k = slot
                if k < SB_PAIRS:
                    if k >= 1:
                        pe.wait_ge(sb_abs, k)
                    for e in range(2):
                        h = 2 * k + e
                        mm(ps[:, e, 0:TP], PROJ[:, C_K + h, 0:P], PROJ[:, C_Q + h, 0:TP], start=True, stop=True)
                        ins = mm(ps[:, e, TP:384], PROJ[:, C_K + h, P:TP], PROJ[:, C_Q + h, P:TP],
                                 start=True, stop=True)
                    ins.then_inc(sb_z, 1)
                k = slot - 2
                if 0 <= k < SB_PAIRS:
                    pe.wait_ge(sb_a, k + 1)
                    if k >= 1:
                        pe.wait_ge(sb_out, k)
                    for e in range(2):
                        cs = slice((2 * k + e) * DH, (2 * k + e + 1) * DH)
                        o = e * TP
                        mm(ps[:, 4, o:o + TP], VTOK[:, 0, cs], SA[:, k % 2, e, 0:TP], start=True, stop=False)
                        ins = mm(ps[:, 4, o + P:o + TP], VTOK[:, 1, cs], SA[:, k % 2, e, TP:384],
                                 start=False, stop=True)
                    ins.then_inc(sb_o, 1)
                k = slot - 1
                if k >= 0:
                    pe.wait_ge(sb_sp, k + 1)
                    if k >= 1:
                        pe.wait_ge(sb_arg, k)
                    if k < SB_PAIRS:
                        for e in range(2):
                            mm(ps[:, 2 + e, 0:384], triu[:, :], SP[:, k % 2, e, :], start=True, stop=False)
                            ins = mm(ps[:, 2 + e, P:TP], ones[:, :], SP[:, k % 2, e, TP:384], start=False, stop=True)
                    else:
                        mm(ps[:, 2, :], triu[:, :], dec_view(SP), start=True, stop=False)
                        ins = mm(ps[:, 2, :], ones[:, :], DR[:, :, :, :].rearrange("p b g h -> p (b g h)"),
                                 start=False, stop=True)
                    ins.then_inc(sb_tail, 1)

            pe.wait_ge(sb_out, SB_PAIRS)
            pe.wait_ge(mod_c, NMC)
            pe.wait_ge(misc_in, 64)
            for h in range(GH):
                mm(ps[:, 4 + h, 0:T], WGU[:, h * DK:(h + 1) * DK], GLOW[:, :], start=True, stop=True).then_inc(g_mm, 1)

            def values(b):
                if b >= 1:
                    pe.wait_ge(v_evac, b)
                for grp in range(2):
                    for half in range(2):
                        for j in range(4):
                            pg = 4 * grp + j
                            if half == 0:
                                pe.wait_ge(vpage_in[pg], 16 * (b + 1))
                            ins = mm(ps[32 * j:32 * j + 32, 4 + half, :], AD[:, b, 32 * grp:32 * grp + 32],
                                     PG[:, pg, half * 512:half * 512 + 512], start=(grp == 0), stop=(grp == 1))
                            if half == 1:
                                ins.then_inc(vpage_used, 1)

            def select(b):
                pe.wait_ge(v_evac, b + 1)
                if b >= 1:
                    pe.wait_ge(v_put, b)
                for h in range(H):
                    ins = mm(ps[:, 6, h:h + 1], DOUT[:, h * DH:(h + 1) * DH], sel_h[:, h:h + 1], start=True, stop=True)
                ins.then_inc(v_sel, 1)

            def dec_products(n):
                h, j = divmod(n, NEV)
                if n >= 1:
                    pe.wait_ge(dec_taken, n)
                if j < PAIRS:
                    if j == 0:
                        pe.wait_ge(km_ready, h + 1)
                    for e in range(2):
                        ins = mm(ps[:, 7, e * DV:(e + 1) * DV], KM[:, 2 * j + e, :], VGS[:, h * DV:(h + 1) * DV],
                                 start=True, stop=True)
                else:
                    for vb in range(VD):
                        for b in range(TS):
                            ins = mm(ps[:, 7, vb * TS + b:vb * TS + b + 1], SS[:, h % 2, b, vb * P:(vb + 1) * P],
                                     QS[:, h, b:b + 1], start=True, stop=True)
                ins.then_inc(dec_mm, 1)

            def tick(i):
                if i in DEC_TICK:
                    dec_products(DEC_TICK[i])
                if i in V_TICK:
                    b = V_TICK[i]
                    if b >= 1:
                        select(b - 1)
                    values(b)

            pe.wait_ge(d_a, 1)
            pe.wait_ge(consts, 4)
            tick(0)
            pe.wait_ge(g_qt, 1 + GH)
            for i in range(1, NSUB):
                pe.wait_ge(g_kd, i)
                kv = kview(i)
                lim = SUB * i
                for h in range(GH):
                    q = QT[:, h, lim:lim + SUB]
                    m0 = min(P, lim)
                    ins = mm(ps[0:m0, h, lim:lim + SUB], kv[:, h, 0:m0], q, start=True, stop=True)
                    if lim > P:
                        ins = mm(ps[0:lim - P, h, P + lim:P + lim + SUB], kv[:, h, P:lim], q, start=True, stop=True)
                ins.then_inc(g_off, 1)
                tick(i)
            pe.wait_ge(g_kd, NSUB)
            pe.wait_ge(g_offev, GH)
            kf = kview(NSUB)
            for j in range(2):
                for i in range(4):
                    h, tb = (4 * j + i) // 2, i % 2
                    ins = tr(ps[:, 2 + j, i * P:(i + 1) * P], kf[:, h, tb * P:(tb + 1) * P], ident[:, :])
                ins.then_inc(g_kft, 1)
            tick(NSUB)
            for t in range(SUB):
                if t == 2 or t == 3:
                    pe.wait_ge(g_kftev, 2)
                    for e in range(2):
                        h = 2 * (t - 2) + e
                        for tb in range(TB):
                            i = 2 * h + tb
                            ins = mm(ps[:, t, e * DV:(e + 1) * DV], KFT[:, i * P:(i + 1) * P],
                                     VG[:, tb, h * DV:(h + 1) * DV], start=(tb == 0), stop=(tb == TB - 1))
                    ins.then_inc(g_st, 1)
                pe.wait_ge(g_dprod, t + 1)
                w = SUB - t
                for e in range(2):
                    n = 2 * NSUB
                    ins = mm(ps[:, e, :].rearrange("p (b n) -> p b n", n=SUB)[:, :, t:SUB],
                             ZSEL[:, SUB - 1 - t:SUB - 1 - t + P],
                             dview(t)[:, e * n:(e + 1) * n, :], start=(t == 0), stop=(t == SUB - 1))
                ins.then_inc(g_diag, 1)
                tick(NSUB + 1 + t)
            pe.wait_ge(g_stev, 2)
            select(TS - 1)
            for h in range(GH):
                pe.wait_ge(g_att, h + 1)
                if h >= 2:
                    pe.wait_ge(g_oev, h - 1)
                at = ATT[:, h, :, :].rearrange("p a b -> p (a b)")
                for vb in range(VD):
                    o = vb * TP
                    cs = slice(h * DV + vb * P, h * DV + (vb + 1) * P)
                    mm(ps[:, 2 + h % 2, o:o + TP], VG[:, 0, cs], at[:, 0:TP], start=True, stop=False)
                    ins = mm(ps[:, 2 + h % 2, o + P:o + TP], VG[:, 1, cs], at[:, TP:384], start=False, stop=True)
                ins.then_inc(g_o, 1)

            for q in range(4):
                pe.wait_ge(msq, q + 1)
                for c in range(4):
                    row = 4 * q + c if q < 2 else H + 2 * (q - 2) + c // 2
                    ins = mm(ps[0:NRM, 4, 0:T], mean_sel[:, q // 2, NRM - 1 - row:2 * NRM - 1 - row],
                             F_LO[:, 4 * q + c, :], start=(q == 0 and c == 0), stop=(q == 3 and c == 3))
            ins.then_inc(msum, 1)
            pe.wait_ge(rs12_ready, 1)
            pe.wait_ge(g_oev, GH)
            for rows, bank in ((range(H, NRM), 4), (range(0, 4), 0), (range(4, H), 4)):
                if rows[0] == 4:
                    pe.wait_ge(norm_sb, 1)
                for c, row in enumerate(rows):
                    ins = mm(ps[:, bank + c, 0:T], ident[0:NRM, row:row + 1].to_broadcast([NRM, P]),
                             rstd[0:NRM, :], start=True, stop=True)
                ins.then_inc(norm_bc, 1)

            pe.wait_ge(h32_ready, 6)
            group(0, W_OUT, NMB, None, 4, None)
            with pe.Fori(1, NOUT) as g:
                group(g, W_OUT, g + NMB, g + NMB, None, lambda m: pe.wait_ge(bank_out, g * MT + (NIN * MT + m - MT + 1)))
            pe.wait_ge(modrow_b, NMB + NOUT)
            mod_turn(modt_b)
            late_sums(SQD, 4, KC - MT)
            sums(SQD, 7, 6, sums_done)

            def ffn_group(g, first):
                nb = g * (2 * UPC) + W_FFN
                for u in range(UPC):
                    if first and u % 2 == 0:
                        pe.wait_ge(h_ready, 8 + u // 2 + 1)
                    unit(u, nb, 0, u == 0, u == UPC - 1,
                         None if first else lambda m: pe.wait_ge(glu_step, g * NGS - 1))
                for u in range(UPC):
                    unit(u + UPC, nb, MT, u == 0, u == UPC - 1,
                         None if first else lambda m: pe.wait_ge(glu_step, g * NGS), k0=2 * u)

            ffn_group(0, True)
            with pe.Fori(1, NFF) as g:
                ffn_group(g, False)

            def down(k, nb, half, first, last, u):
                pe.wait_ge(lo_ready, nb + (u + 1))
                if half == 0 and u == 0:
                    pe.wait_ge(glu_done, (nb - W_DOWN) // 4 + 1 if isinstance(nb, int) else DONE[0])
                for m in range(8):
                    if first:
                        if half == 0:
                            pe.wait_ge(glu_step, NFF * NGS - 1 if m < MT else NFF * NGS)
                        else:
                            pe.wait_ge(bank_out, (NIN + NOUT) * MT + m + 1)
                    cs = slice(m * P, (m + 1) * P)
                    xh = A_HI[:, bass.ds(k, 1), :].rearrange("p o t -> p (o t)")
                    xl = A_LO[:, bass.ds(k, 1), :].rearrange("p o t -> p (o t)")
                    out = ps[:, m, 0:T]
                    mm(out, HI[:, u, cs], xh, start=first, stop=False)
                    mm(out, HI[:, u, cs], xl, start=False, stop=False)
                    ins = mm(out, LO[:, u, cs], xh, start=False, stop=last)
                    if last and m < 7:
                        ins.then_inc(bank_done, 1)
                ins.then_inc(unit_used, 1)

            DONE = [None]
            for half in range(2):
                w0 = W_DOWN + half * FC
                for u in range(4):
                    down(u, w0, half, u == 0, False, u)
                with pe.Fori(1, FC // 4 - 1) as j:
                    DONE[0] = j + 1
                    for u in range(4):
                        down(j * 4 + u, j * 4 + w0, half, False, False, u)
                for u in range(4):
                    down(FC - 4 + u, w0 + FC - 4, half, False, u == 3, u)

            pe.wait_ge(bank_out, MT * (NIN + NOUT) + KC)
            late_sums(F_LO, 10, KC // 2)
            n = 0
            for q in range(4):
                pe.wait_ge(x_new, 4 + q + 1)
                for t0, nt, dst in y_jobs:
                    if n >= 4:
                        pe.wait_ge(y_rows, n - 3)
                    for i in range(4):
                        ins = tr(ps[0:nt, 2 + n % 4, i * P:(i + 1) * P], X[:, 4 * q + i, t0:t0 + nt], ident[:, :])
                    ins.then_inc(y_tr, 1)
                    n += 1


_INS = ["x_prompt", "x_sample", "c_prompt", "c_sample", "cache_k", "cache_v", "page_table", "state_gla", "w_ada",
        "b_ada", "g_pre_mix", "w_in", "b_sb", "w_gate_up", "b_gate", "g_sb_out", "g_gla_out", "w_out", "g_post_mix",
        "g_pre_ffn", "w_ffn_gate", "w_ffn_up", "w_ffn_down", "g_post_ffn"]


def kernel(**inputs):
    import numpy as np
    import concourse.bacc as bacc
    from concourse.bass_utils import run_bass_kernel_spmd as run

    nc = bacc.Bacc("TRN2", target_bir_lowering=False, num_devices=1)
    arrays, args = {}, []
    for name in _INS:
        a = np.ascontiguousarray(inputs[name])
        arrays[f"in_{name}"] = a
        args.append(nc.dram_tensor(f"in_{name}", a.shape, mybir.dt.from_np(a.dtype), kind="ExternalInput").ap())
    batch, seq, width = inputs["x_prompt"].shape
    rows = inputs["x_sample"].shape[0]
    depth, _, _, heads, head_dim = inputs["cache_k"].shape
    gla = inputs["state_gla"].shape[2:]
    outs = [(batch, seq, width), (rows, 1, width),
            (depth, batch, seq, heads, head_dim), (depth, batch, seq, heads, head_dim), (depth, batch, *gla),
            (depth, rows, 1, heads, head_dim), (depth, rows, 1, heads, head_dim), (depth, rows, *gla)]
    for i, shape in enumerate(outs):
        args.append(nc.dram_tensor(f"out_{i}", shape, F32, kind="ExternalOutput").ap())
    stickbreak_gla_layer(nc, *args)
    r = run(nc, [arrays], core_ids=[0])
    return tuple(r.results[0][f"out_{i}"] for i in range(len(outs)))
```
